# Optimizing a Trainium2 kernel written in Bass

```python
import jax, jax.numpy as jnp
from jax import lax
import numpy as np

D_MODEL = 1024
BATCH = 1
SEQ = 512
DEPTH = 1

HEAD_DIM = 64
N_MIX_HEADS = D_MODEL // HEAD_DIM
A_Q_HEADS = N_MIX_HEADS // 2
A_KV_HEADS = max(1, A_Q_HEADS // 4)
A_HALF_WINDOW = 128
B_HEADS = N_MIX_HEADS - A_Q_HEADS
B_BRANCHES = ((128, 1), (512, 4), (2048, 16))
ATTN_BLOCK = 128
N_ALIBI_HEADS = A_Q_HEADS + B_HEADS
A_Q_W = A_Q_HEADS * HEAD_DIM
A_KV_W = A_KV_HEADS * HEAD_DIM
B_W = B_HEADS * HEAD_DIM
IN_PROJ_W = A_Q_W + 2 * A_KV_W + 3 * B_W
MIX_W = A_Q_W + B_W
N_EXPERTS = 32
TOP_K = 4
D_FF = D_MODEL
SWIGLU_ALPHA = 1.702
SWIGLU_LIMIT = 7.0
MOE_ROW_BLOCK = 128
NORM_EPS = 1e-5
MASK_VALUE = -1e30

kernel_name = "hymba_style_sink_gqa_dilated_moe_encoder"

def rms_norm(x, g):
    xf = x.astype(jnp.float32)
    y = xf * lax.rsqrt(jnp.mean(xf * xf, axis=-1, keepdims=True) + NORM_EPS)
    return (y * g.astype(jnp.float32)).astype(x.dtype)

def alibi_slopes(n):
    return jnp.exp2(-8.0 * jnp.arange(1, n + 1, dtype=jnp.float32) / n)

def banded_attention(q, k, v, half_w, dist_scale, slopes, sink=None):
    n, h, r, L, hd = q.shape
    blk = min(ATTN_BLOCK, L)
    nb = -(-L // blk)
    lp = nb * blk
    kw = blk + 2 * half_w
    qb = jnp.pad(q, ((0, 0), (0, 0), (0, 0), (0, lp - L), (0, 0))).reshape(n, h, r, nb, blk, hd)
    pad_k = ((0, 0), (0, 0), (half_w, lp - L + half_w), (0, 0))
    kidx = jnp.arange(nb)[:, None] * blk + jnp.arange(kw)[None, :]
    kb = jnp.pad(k, pad_k)[:, :, kidx]
    vb = jnp.pad(v, pad_k)[:, :, kidx]
    s = jnp.einsum('nhrbqd,nhbkd->nhrbqk', qb, kb).astype(jnp.float32) * (hd ** -0.5)
    qpos = jnp.arange(nb)[:, None] * blk + jnp.arange(blk)[None, :]
    kpos = kidx - half_w
    dist = jnp.abs(qpos[:, :, None] - kpos[:, None, :])
    valid = (dist <= half_w) & (kpos >= 0)[:, None, :] & (kpos < L)[:, None, :]
    bias = -slopes.astype(jnp.float32)[:, :, None, None, None] * (dist * dist_scale).astype(jnp.float32)
    s = jnp.where(valid, s + bias, MASK_VALUE)
    m = jnp.max(s, axis=-1)
    if sink is not None:
        sink_f = sink.astype(jnp.float32)[:, :, None, None]
        m = jnp.maximum(m, sink_f)
    p = jnp.exp(s - m[..., None])
    denom = jnp.sum(p, axis=-1)
    if sink is not None:
        denom = denom + jnp.exp(sink_f - m)
    o = jnp.einsum('nhrbqk,nhbkd->nhrbqd', p, vb.astype(jnp.float32)) / denom[..., None]
    o = o.reshape(n, h, r, lp, hd)[:, :, :, :L].astype(q.dtype)
    lse = (m + jnp.log(denom)).reshape(n, h, r, lp)[..., :L]
    return o, lse

def windowed_sink_gqa(q, k, v, q_gain, k_gain, sinks, slopes):
    b, s, hq, hd = q.shape
    hkv = k.shape[2]
    r = hq // hkv
    q = rms_norm(q, q_gain)
    k = rms_norm(k, k_gain)
    qh = q.reshape(b, s, hkv, r, hd).transpose(0, 2, 3, 1, 4)
    kh = k.transpose(0, 2, 1, 3)
    vh = v.transpose(0, 2, 1, 3)
    o, _ = banded_attention(qh, kh, vh, A_HALF_WINDOW, 1,
                            slopes.reshape(hkv, r), sinks.reshape(hkv, r))
    return o.transpose(0, 3, 1, 2, 4).reshape(b, s, hq * hd)

def to_strided(t, dil):
    b, s, h, hd = t.shape
    return t.reshape(b, s // dil, dil, h, hd).transpose(0, 2, 3, 1, 4).reshape(b * dil, h, s // dil, hd)

def dilated_attention(q, k, v, q_gain, k_gain, slopes):
    b, s, h, hd = q.shape
    q = rms_norm(q, q_gain)
    k = rms_norm(k, k_gain)
    outs, lses = [], []
    for window, dil in B_BRANCHES:
        L = s // dil
        o, lse = banded_attention(to_strided(q, dil)[:, :, None], to_strided(k, dil),
                                  to_strided(v, dil), window // (2 * dil), dil, slopes[:, None])
        o = o[:, :, 0].reshape(b, dil, h, L, hd).transpose(0, 3, 1, 2, 4).reshape(b, s, h, hd)
        lse = lse[:, :, 0].reshape(b, dil, h, L).transpose(0, 3, 1, 2).reshape(b, s, h)
        outs.append(o.astype(jnp.float32))
        lses.append(lse)
    w = jax.nn.softmax(jnp.stack(lses), axis=0)
    o = jnp.sum(w[..., None] * jnp.stack(outs), axis=0)
    return o.reshape(b, s, h * hd).astype(q.dtype)

def moe_ffn(h, w_router, b_router, w1, b1, w2, b2):
    bsz, s, d = h.shape
    n = bsz * s
    g = MOE_ROW_BLOCK
    hf = h.reshape(n, d)
    logits = (hf @ w_router).astype(jnp.float32) + b_router.astype(jnp.float32)
    top_v, top_i = lax.top_k(logits, TOP_K)
    gates = jax.nn.softmax(top_v, axis=-1)
    nk = n * TOP_K
    flat_e = top_i.reshape(nk)
    flat_tok = jnp.repeat(jnp.arange(n, dtype=jnp.int32), TOP_K)
    order = jnp.argsort(flat_e)
    se = flat_e[order]
    stok = flat_tok[order]
    sgate = gates.reshape(nk)[order]
    counts = jnp.bincount(flat_e, length=N_EXPERTS)
    starts = jnp.cumsum(counts) - counts
    pcounts = (counts + g - 1) // g * g
    pends = jnp.cumsum(pcounts)
    pstarts = pends - pcounts
    dest = pstarts[se] + jnp.arange(nk, dtype=jnp.int32) - starts[se]
    n_rows = nk + N_EXPERTS * g
    n_blk = n_rows // g
    row_tok = jnp.zeros((n_rows,), jnp.int32).at[dest].set(stok)
    blk_exp = jnp.minimum(jnp.searchsorted(pends, jnp.arange(n_blk, dtype=jnp.int32) * g, side='right'),
                          N_EXPERTS - 1)
    xb = hf[row_tok].reshape(n_blk, g, d)

    def expert_block(args):
        xg, e = args
        a = xg @ w1[e] + b1[e]
        glu, lin = a[:, :D_FF], a[:, D_FF:]
        glu = jnp.minimum(glu, SWIGLU_LIMIT)
        lin = jnp.clip(lin, -SWIGLU_LIMIT, SWIGLU_LIMIT)
        act = glu * jax.nn.sigmoid(SWIGLU_ALPHA * glu) * (lin + 1)
        return act @ w2[e] + b2[e]

    y = lax.map(expert_block, (xb, blk_exp)).reshape(n_rows, d)
    contrib = y[dest] * sgate[:, None].astype(y.dtype)
    return jax.ops.segment_sum(contrib, stok, num_segments=n).reshape(bsz, s, d)

def setup_inputs(seed: int = 0) -> dict:
    key = jax.random.key(seed)
    ks = jax.random.split(key, 16)
    f32 = jnp.float32
    nrm = lambda k, shape, sc: jax.random.normal(k, shape, f32) * sc
    return {
        "x": jax.random.normal(ks[0], (BATCH, SEQ, D_MODEL), f32),
        "attn_norm_g": 1.0 + nrm(ks[1], (DEPTH, D_MODEL), 0.02),
        "w_in": nrm(ks[2], (DEPTH, D_MODEL, IN_PROJ_W), D_MODEL ** -0.5),
        "a_q_norm_g": 1.0 + nrm(ks[3], (DEPTH, HEAD_DIM), 0.02),
        "a_k_norm_g": 1.0 + nrm(ks[4], (DEPTH, HEAD_DIM), 0.02),
        "a_sinks": nrm(ks[5], (DEPTH, A_Q_HEADS), 0.5),
        "b_q_norm_g": 1.0 + nrm(ks[6], (DEPTH, HEAD_DIM), 0.02),
        "b_k_norm_g": 1.0 + nrm(ks[7], (DEPTH, HEAD_DIM), 0.02),
        "w_out": nrm(ks[8], (DEPTH, MIX_W, D_MODEL), MIX_W ** -0.5),
        "ffn_norm_g": 1.0 + nrm(ks[9], (DEPTH, D_MODEL), 0.02),
        "w_router": nrm(ks[10], (DEPTH, D_MODEL, N_EXPERTS), D_MODEL ** -0.5),
        "b_router": nrm(ks[11], (DEPTH, N_EXPERTS), 0.01),
        "w1": nrm(ks[12], (DEPTH, N_EXPERTS, D_MODEL, 2 * D_FF), D_MODEL ** -0.5),
        "b1": nrm(ks[13], (DEPTH, N_EXPERTS, 2 * D_FF), 0.02),
        "w2": nrm(ks[14], (DEPTH, N_EXPERTS, D_FF, D_MODEL), D_FF ** -0.5),
        "b2": nrm(ks[15], (DEPTH, N_EXPERTS, D_MODEL), 0.02),
    }

def reference(x, attn_norm_g, w_in, a_q_norm_g, a_k_norm_g, a_sinks, b_q_norm_g, b_k_norm_g,
              w_out, ffn_norm_g, w_router, b_router, w1, b1, w2, b2):
    bsz, s, _ = x.shape
    slopes = alibi_slopes(N_ALIBI_HEADS)
    slopes_a = slopes[:A_Q_HEADS]
    slopes_b = slopes[A_Q_HEADS:]
    splits = np.cumsum([A_Q_W, A_KV_W, A_KV_W, B_W, B_W]).tolist()
    for i in range(DEPTH):
        hn = rms_norm(x, attn_norm_g[i])
        proj = hn @ w_in[i]
        qa, ka, va, qb, kb, vb = jnp.split(proj, splits, axis=-1)
        out_a = windowed_sink_gqa(qa.reshape(bsz, s, A_Q_HEADS, HEAD_DIM),
                                  ka.reshape(bsz, s, A_KV_HEADS, HEAD_DIM),
                                  va.reshape(bsz, s, A_KV_HEADS, HEAD_DIM),
                                  a_q_norm_g[i], a_k_norm_g[i], a_sinks[i], slopes_a)
        out_b = dilated_attention(qb.reshape(bsz, s, B_HEADS, HEAD_DIM),
                                  kb.reshape(bsz, s, B_HEADS, HEAD_DIM),
                                  vb.reshape(bsz, s, B_HEADS, HEAD_DIM),
                                  b_q_norm_g[i], b_k_norm_g[i], slopes_b)
        x = x + jnp.concatenate([out_a, out_b], axis=-1) @ w_out[i]
        hf = rms_norm(x, ffn_norm_g[i])
        x = x + moe_ffn(hf, w_router[i], b_router[i], w1[i], b1[i], w2[i], b2[i])
    return x


_drawn_inputs = setup_inputs


def setup_inputs(seed=0):
    import zlib

    import numpy as np

    out = dict(_drawn_inputs(seed))
    spreads = {}
    factors = {'a_k_norm_g': 3.202,
     'b_q_norm_g': 4.249,
     'b_k_norm_g': 4.629,
     'b1': 5.177,
     'b2': 5.994,
     'a_sinks': 3.401}
    for name, (base, spread) in spreads.items():
        noise = np.random.default_rng([zlib.crc32(name.encode()), seed]).standard_normal(out[name].shape)
        drawn = base * np.exp(spread * noise) if base else spread * noise
        out[name] = __import__('jax').numpy.asarray(drawn.astype(out[name].dtype))
    for name, factor in factors.items():
        out[name] = (out[name] * factor).astype(out[name].dtype)
    return out
```

```python
from contextlib import ExitStack

import concourse.bass as bass
from concourse import mybir

F32 = mybir.dt.float32
F32R = mybir.dt.float32r
I32 = mybir.dt.int32
U32 = mybir.dt.uint32
ALU = mybir.AluOpType
ACT = mybir.ActivationFunctionType
AX = mybir.AxisListType

P = 128
SEQ = 512
D = 1024
NT = SEQ // P
ND = D // P
HD = 64
AQ, AKV, BH = 8, 2, 8
NE, TOPK, FF = 32, 4, 1024
EPS = 1e-5
LIMIT, ALPHA = 7.0, 1.702
NEG = -1e30
A_HALF = 128
BRANCHES = ((128, 1), (512, 4), (2048, 16))
LN2, LN3 = 0.6931471805599453, 1.0986122886681098

BLOCKS = ((0, 512), (512, 768), (768, 1280), (1280, 1792), (1792, 2304))
NORMED = (512, 128, 512, 512)
PROJ_W = 2304
VA, VB, ATT = 640, 1792, 768

NP = 8
UN = 8
CH = 12
W1C = 8
RAW, PARTS = 6, 3
POOL_LO = (3, 6, 9)
OVER = 16
GC = NE + OVER + 1
KB = 1024


def lo_before(c, pool):
    return sum((k in POOL_LO) == pool for k in range(c + 1))


def layer(nc, x, attn_norm_g, w_in, a_q_norm_g, a_k_norm_g, a_sinks, b_q_norm_g, b_k_norm_g,
          w_out, ffn_norm_g, w_router, b_router, w1, b1, w2, b2, out):
    ctx = ExitStack()
    with ctx:
        def at(name, shape, dt, offset):
            return nc.alloc_sbuf_tensor_at(name, shape, dt, offset=64 + offset)

        acc = at("acc", [P, NT, D], F32, 0)
        raw = at("raw", [P, RAW, 2048], F32, 16 * KB)
        c0 = 64 * KB
        ident = at("ident", [P, P], F32, c0)
        slot_iota = at("slot_iota", [P, P], F32, c0 + 512)
        ones = at("ones", [P, P], F32, c0 + 1024)
        before = at("before", [P, P], F32, c0 + 1536)
        wr = at("wr", [P, ND, NE], F32, c0 + 2048)
        gate_t = at("gate_t", [P, NT, GC], F32, c0 + 3072)
        pos_t = at("pos_t", [P, NT, GC], F32, c0 + 3872)
        c1 = c0 + 4672
        br_b = at("br_b", [P, NE], F32, c1)
        sinks = at("sinks", [P, AQ], F32, c1 + 128)
        nslope = at("nslope", [P, 2 * NP], F32, c1 + 160)
        head_g = at("head_g", [P, 4], F32, c1 + 224)
        half_pow = at("half_pow", [P, P], F32, c1 + 256)
        stat = at("stat", [P, 16], F32, c1 + 768)
        over_i = at("over_i", [1, OVER + 1], I32, c1 + 832)
        bias_sel = at("bias_sel", [2 * NE, P], F32R, c1 + 928)
        row_number = at("row_number", [2 * NE, 1], F32, c1 + 1440)
        item_row = at("item_row", [2 * NE, GC], F32, c1 + 1472)

        r1 = 71 * KB
        qkv = at("qkv", [P, NT, PROJ_W], F32, r1)
        qta = at("qta", [P, 4, SEQ], F32, r1 + 36864)
        kta = at("kta", [P, SEQ], F32, r1 + 45056)
        qtb = at("qtb", [P, 4, SEQ], F32, r1 + 47104)
        ktb = at("ktb", [P, 4, SEQ], F32, r1 + 55296)
        dist = at("dist", [P, 896], F32, r1 + 63488)
        log_a = at("log_a", [P, 896], F32, r1 + 67072)
        log_b = at("log_b", [P, 896], F32, r1 + 70656)
        table = at("table", [P, 2, 2, 896], F32, r1 + 74240)
        delta_i = at("delta_i", [P, 896], I32, r1 + 74240)
        low_i = at("low_i", [P, 896], I32, r1 + 74240 + 3584)
        tmp_a = at("tmp_a", [P, 896], F32, r1 + 74240 + 7168)
        tmp_b = at("tmp_b", [P, 896], F32, r1 + 74240 + 10752)
        sumsq = at("sumsq", [P, 4, NT, 8], F32, r1 + 88576)
        maxes = at("maxes", [P, 16], F32, r1 + 89088)
        neg_max = at("neg_max", [P, 16], F32, r1 + 89152)
        den = at("den", [P, 16], F32, r1 + 89216)
        sink_d = at("sink_d", [P, 16], F32, r1 + 89280)
        sink_e = at("sink_e", [P, 16], F32, r1 + 89344)
        recip = at("recip", [P, 16], F32, r1 + 89408)
        slope2 = at("slope2", [P, 2], F32, r1 + 89472)
        gain_rows = at("gain_rows", [4, P], F32, r1 + 89504)
        norm_out = at("norm_out", [P, 2, 512], F32, r1 + 36864)
        bias_raw = at("bias_raw", [2 * NE, 3072], F32, r1 + 57344)
        hf_hi = at("hf_hi", [P, NT, D], F32R, r1)
        hf_lo = at("hf_lo", [P, NT, D], F32R, r1 + 16384)
        w_hi = at("w_hi", [P, PARTS, 2048], F32R, r1 + 32768)
        w_lo = at("w_lo", [P, PARTS, 2048], F32R, r1 + 57344)
        y_hi = at("y_hi", [P, D], F32R, r1 + 81920)
        y_lo = at("y_lo", [P, D], F32R, r1 + 86016)

        r2 = r1 + 90 * KB
        xn = at("xn", [P, NT, D], F32, r2)
        xt = at("xt", [P, ND, SEQ], F32, r2 + 16384)
        gain_b = at("gain_b", [P, 2, D], F32, r2 + 32768)
        squares = at("squares", [P, 2, 512], F32, r2)
        probs = at("probs", [P, 4, 512], F32, r2)
        probs_t = at("probs_t", [P, 2, 512], F32, r2 + 8192)
        q_st = at("q_st", [P, 2, SEQ], F32, r2 + 12288)
        k_st = at("k_st", [P, 2, SEQ], F32, r2 + 16384)
        hf = at("hf", [P, NT, D], F32, r2)
        rows = at("rows", [1, 2, D], F32, r2 + 40960)
        x_hi = at("x_hi", [P, ND, P], F32R, r2)
        x_lo = at("x_lo", [P, ND, P], F32R, r2 + 4096)
        glu = at("glu", [P, FF], F32, r2 + 8192)
        lin = at("lin", [P, FF], F32, r2 + 12288)
        sig = at("sig", [P, FF], F32, r2 + 16384)
        act_hi = at("act_hi", [P, ND, P], F32R, r2 + 20480)
        act_lo = at("act_lo", [P, ND, P], F32R, r2 + 24576)
        sel = at("sel", [P, NT, P], F32R, r2 + 28672)
        sel_next = at("sel_next", [P, SEQ], F32R, r2 + 30720)
        sel_now = at("sel_now", [P, SEQ], F32R, r2 + 32768)
        bias_rows = at("bias_rows", [2 * NE, 3072], F32R, r2 + 34816)
        r3 = r2 + 49152
        chosen = at("chosen", [P, 16, NE], F32, r3)
        weighed = at("weighed", [P, 16, NE], F32, r3 + 2048)
        logits = at("logits", [P, NT, NE], F32, r3 + 4096)
        mask = at("mask", [P, NT, NE], F32, r3 + 4608)
        top = at("top", [P, NT, 8], F32, r3 + 5120)
        top_i = at("top_i", [P, NT, 8], U32, r3 + 5248)
        top_e = at("top_e", [P, NT, TOPK], F32, r3 + 5376)
        top_w = at("top_w", [P, NT, TOPK], F32, r3 + 5440)
        top_s = at("top_s", [P, NT], F32, r3 + 5504)
        top_r = at("top_r", [P, NT], F32, r3 + 5536)
        pos_e = at("pos_e", [NE, SEQ], F32, r3 + 5568)
        gate_e = at("gate_e", [NE, SEQ], F32, r3 + 7616)
        r4 = r3 + 9664
        count = at("count", [NE, 1], F32, r4)
        more = at("more", [NE, 4], F32, r4 + 32)
        item_in = at("item_in", [NE, OVER], F32, r4 + 64)
        item_sh = at("item_sh", [NE, OVER], F32, r4 + 128)
        item_tm = at("item_tm", [NE, OVER], F32, r4 + 192)
        e_iota = at("e_iota", [NE, 1], F32, r4 + 256)
        neg_ones = at("neg_ones", [NE, P], F32, r4 + 288)
        over_f = at("over_f", [1, OVER + 1], F32, r4 + 800)

        ps = ctx.enter_context(nc.psum_tensor("ps", [P, 8 * 512], F32))

        def bank(b, n=1):
            return ps[:, b * 512:(b + n) * 512]

        def sem(name):
            return ctx.enter_context(nc.semaphore(name))

        x_in = [sem(f"x_in{t}") for t in range(NT)]
        rows_in, small_in, router_in = sem("rows_in"), sem("small_in"), sem("router_in")
        win_in = [sem(f"win_in{b}") for b in range(3)]
        bias_in, wout_in, out_stored = sem("bias_in"), sem("wout_in"), sem("out_stored")
        raw_in = [sem(f"raw_in{s}") for s in range(RAW)]

        ident_ready, consts_ready, pool_step = sem("ident_ready"), sem("consts_ready"), sem("pool_step")
        dve_step = sem("dve_step")
        bias_split_hi, bias_split_lo = sem("bias_split_hi"), sem("bias_split_lo")
        gain_rep, gain_copied = sem("gain_rep"), sem("gain_copied")
        sq_x, var_x, rstd_x, xn_ready = sem("sq_x"), sem("var_x"), sem("rstd_x"), sem("xn_ready")
        xt_turned = sem("xt_turned")
        xt_copied = [sem("xt_copied_act"), sem("xt_copied_dve")]
        head_turned, head_ready = sem("head_turned"), sem("head_ready")
        win_used, qkv_done, qkv_copied = sem("win_used"), sem("qkv_done"), sem("qkv_copied")
        sq_done, sq_read = sem("sq_done"), sem("sq_read")
        var_q, rstd_q, qk_normed = sem("var_q"), sem("rstd_q"), sem("qk_normed")
        qkt_turned = sem("qkt_turned")
        qkt_copied = [sem("qkt_copied_act"), sem("qkt_copied_dve")]
        delta_ready, tables_ready = sem("delta_ready"), sem("tables_ready")
        staged, slope_ready, scaled, bias_ready = sem("staged"), sem("slope_ready"), sem("scaled"), sem("bias_ready")
        scored, scores_read, max_ready, exp_done = sem("scored"), sem("scores_read"), sem("max_ready"), sem("exp_done")
        turned, pv_done, o_read = sem("turned"), sem("pv_done"), sem("o_read")
        pt_copied = [sem("pt_copied_act"), sem("pt_copied_dve")]
        sink_d_ready, sink_e_ready, den_ready, recip_ready = (
            sem("sink_d_ready"), sem("sink_e_ready"), sem("den_ready"), sem("recip_ready"))
        att_turned = sem("att_turned")
        att_copied = [sem("att_copied_act"), sem("att_copied_dve")]
        out_done, x1_done = sem("out_done"), sem("x1_done")
        sq_1, var_1, rstd_1, hf_ready = sem("sq_1"), sem("var_1"), sem("rstd_1"), sem("hf_ready")
        hf_hi_done, hf_lo_done, hf_turned = sem("hf_hi_done"), sem("hf_lo_done"), sem("hf_turned")
        hf_copied = [sem("hf_copied_act"), sem("hf_copied_dve")]
        logits_done = sem("logits_done")
        gap_ready, gap_exp = sem("gap_ready"), sem("gap_exp")
        mask_ready, pos_done, count_done = sem("mask_ready"), sem("pos_done"), sem("count_done")
        e_turned = sem("e_turned")
        more_ready, first_done, lists_ready = sem("more_ready"), sem("first_done"), sem("lists_ready")
        over_done, over_ready = sem("over_done"), sem("over_ready")

        hi_done, parts_free = sem("hi_done"), sem("parts_free")
        lo_done = [sem("lo_done_dve"), sem("lo_done_pool")]
        bias_sel_ready, bias_used = sem("bias_sel_ready"), sem("bias_used")
        glu_ready, lin_ready, sig_ready = sem("glu_ready"), sem("lin_ready"), sem("sig_ready")
        prod_ready, act_ready = sem("prod_ready"), sem("act_ready")
        act_turned, act_hi_done, act_lo_done = sem("act_turned"), sem("act_hi_done"), sem("act_lo_done")
        y_zeroed, y_hi_done, y_lo_done = sem("y_zeroed"), sem("y_hi_done"), sem("y_lo_done")
        sel_ready, sel_turned, sel_moved, selt_done = sem("sel_ready"), sem("sel_turned"), sem("sel_moved"), sem("selt_done")
        gathered, xg_done = sem("gathered"), sem("xg_done")
        combined, acc_done = sem("combined"), sem("acc_done")

        block = ctx.enter_context(nc.Block())

        win_v = w_in[0].rearrange("(k p) n -> p k n", p=P)

        def win_sb(b):
            w = BLOCKS[b][1] - BLOCKS[b][0]
            s = 2 * (b % 3)
            return raw[:, s:s + 2, :].rearrange("p s n -> p (s n)")[:, 0:ND * w].rearrange("p (k n) -> p k n", k=ND)

        wout_sb = raw[:, 2:6, :].rearrange("p s n -> p (s n)").rearrange("p (k n) -> p k n", k=ND)

        def paired(b, ap):
            return ap.rearrange("p (j g d) -> p g j d", g=2, d=HD) if b == 0 else ap

        def banked(b, ap):
            return ap.rearrange("p (g j d) -> p g j d", g=2, d=HD) if b == 0 else ap

        def keys(kind, i):
            return (max(0, i - 1), min(NT, i + 2)) if kind == "a" else (0, NT)

        @block.sync
        def _(sp):
            for t in range(NT):
                sp.dma_start(acc[:, t, :], x[0, t * P:(t + 1) * P, :]).then_inc(x_in[t], 16)
            sp.dma_start(rows[:, 0, :], attn_norm_g).then_inc(rows_in, 16)
            sp.dma_start(rows[:, 1, :], ffn_norm_g).then_inc(rows_in, 16)

            def load_win(b):
                sp.dma_start(win_sb(b), win_v[:, :, BLOCKS[b][0]:BLOCKS[b][1]]).then_inc(win_in[b % 3], 16)

            load_win(0)
            for j, g in enumerate((a_q_norm_g, a_k_norm_g, b_q_norm_g, b_k_norm_g)):
                for h in range(2):
                    sp.dma_start(gain_rows[j:j + 1, h * HD:(h + 1) * HD], g).then_inc(small_in, 16)
            sp.dma_start(sinks[:, :], a_sinks.to_broadcast([P, AQ])).then_inc(small_in, 16)
            sp.dma_start(br_b[:, :], b_router.to_broadcast([P, NE])).then_inc(small_in, 16)
            load_win(1)
            load_win(2)
            sp.dma_start(wr[:, :, :], w_router[0].rearrange("(k p) e -> p k e", p=P)).then_inc(router_in, 16)
            for b in (3, 4):
                sp.wait_ge(win_used, b - 2)
                load_win(b)

            def load_chunk(e, c):
                if c < W1C:
                    src, dst = w1[0, e, c * P:(c + 1) * P, :], raw[:, c % RAW, :]
                else:
                    k = (c - W1C) * 2 * P
                    src = w2[0, e, k:k + 2 * P, :].rearrange("(j p) n -> p j n", p=P)
                    dst = raw[:, c % RAW, :].rearrange("p (j n) -> p j n", j=2)
                sp.dma_start(dst, src).then_inc(raw_in[c % RAW], 16)

            sp.wait_ge(win_used, 4)
            for c in range(2):
                load_chunk(0, c)
            sp.wait_ge(win_used, 5)
            sp.dma_start(wout_sb, w_out[0].rearrange("(k p) n -> p k n", p=P)).then_inc(wout_in, 16)
            sp.wait_ge(att_turned, 2 * NT)
            for h in range(2):
                sp.dma_start(bias_raw[h * NE:(h + 1) * NE, 0:2048], b1[0]).then_inc(bias_in, 16)
                sp.dma_start(bias_raw[h * NE:(h + 1) * NE, 2048:3072], b2[0]).then_inc(bias_in, 16)
            sp.wait_ge(out_done, 2 * NT)
            for c in range(2, RAW):
                load_chunk(0, c)

            def chunk_split(i, c):
                pool = c in POOL_LO
                n = len(POOL_LO) if pool else CH - len(POOL_LO)
                sp.wait_ge(lo_done[pool], i * n + lo_before(c, pool))

            with sp.Fori(0, NE - 1) as i:
                for c in range(RAW, CH):
                    chunk_split(i, c - RAW)
                    if c < W1C:
                        src, dst = w1[0, bass.ds(i, 1), c * P:(c + 1) * P, :].rearrange("e p n -> (e p) n"), raw[:, c % RAW, :]
                    else:
                        k = (c - W1C) * 2 * P
                        src = w2[0, bass.ds(i, 1), k:k + 2 * P, :].rearrange("e (j p) n -> p (e j) n", p=P)
                        dst = raw[:, c % RAW, :].rearrange("p (j n) -> p j n", j=2)
                    sp.dma_start(dst, src).then_inc(raw_in[c % RAW], 16)
                for c in range(RAW):
                    chunk_split(i, c + RAW)
                    sp.dma_start(raw[:, c, :], w1[0, bass.ds(i + 1, 1), c * P:(c + 1) * P, :].rearrange("e p n -> (e p) n")
                                 ).then_inc(raw_in[c], 16)
            for c in range(RAW, CH):
                chunk_split(NE - 1, c - RAW)
                load_chunk(NE - 1, c)

            sp.wait_ge(over_ready, 1)
            n_items = sp.value_load(over_i[0:1, OVER:OVER + 1], min_val=NE, max_val=NE + OVER)
            with sp.If(n_items > NE):
                with sp.Fori(NE, n_items) as i:
                    e = sp.value_load(over_i[0:1, bass.ds(i - NE, 1)], min_val=0, max_val=NE - 1)
                    for c in range(CH):
                        if c < RAW:
                            chunk_split(i - 1, c + RAW)
                        else:
                            chunk_split(i, c - RAW)
                        if c < W1C:
                            src, dst = w1[0, bass.ds(e, 1), c * P:(c + 1) * P, :].rearrange("e p n -> (e p) n"), raw[:, c % RAW, :]
                        else:
                            k = (c - W1C) * 2 * P
                            src = w2[0, bass.ds(e, 1), k:k + 2 * P, :].rearrange("e (j p) n -> p (e j) n", p=P)
                            dst = raw[:, c % RAW, :].rearrange("p (j n) -> p j n", j=2)
                        sp.dma_start(dst, src).then_inc(raw_in[c % RAW], 16)
            for t in range(NT):
                sp.wait_ge(acc_done, n_items * 8 + 2 * t + 2)
                sp.dma_start(out[0, t * P:(t + 1) * P, :], acc[:, t, :]).then_inc(out_stored, 16)
            sp.wait_ge(out_stored, 16 * NT)

        @block.gpsimd
        def _(pool):
            pool.memset(ident[:, :], 0.0).then_inc(pool_step, 1)
            pool.memset(before[:, :], 0.0).then_inc(pool_step, 1)
            pool.memset(half_pow[:, :], -0.5).then_inc(ident_ready, 1)
            pool.wait_ge(pool_step, 2)
            pool.affine_select(out=ident[:, :], in_=ident[:, :], compare_op=ALU.not_equal, fill=1.0, base=0,
                               pattern=[[-1, P]], channel_multiplier=1).then_inc(ident_ready, 1)
            pool.affine_select(out=before[:, :], in_=before[:, :], compare_op=ALU.is_ge, fill=1.0, base=0,
                               pattern=[[-1, P]], channel_multiplier=1).then_inc(consts_ready, 1)
            pool.memset(ones[:, :], 1.0).then_inc(ident_ready, 1)
            pool.iota(slot_iota[:, :], pattern=[[1, P]], base=0, channel_multiplier=0,
                      allow_small_or_imprecise_dtypes=True).then_inc(consts_ready, 1)
            pool.iota(e_iota[:, :], pattern=[[1, 1]], base=0, channel_multiplier=1,
                      allow_small_or_imprecise_dtypes=True).then_inc(consts_ready, 1)
            pool.iota(row_number[:, :], pattern=[[1, 1]], base=0, channel_multiplier=1,
                      allow_small_or_imprecise_dtypes=True).then_inc(consts_ready, 1)
            pool.memset(neg_ones[:, :], -1.0).then_inc(consts_ready, 1)
            pool.iota(delta_i[:, :], pattern=[[1, 896]], base=-384, channel_multiplier=-1).then_inc(delta_ready, 1)
            for r in range(NP):
                for hh in range(2):
                    head = (r + 4 * hh) if r < 4 else (8 + 2 * (r - 4) + hh)
                    pool.memset(nslope[:, 2 * r + hh:2 * r + hh + 1], -(2.0 ** (-8.0 * (head + 1) / 16))
                                ).then_inc(pool_step, 1)
            for t in range(NT):
                pool.wait_ge(var_x, t + 1)
                pool.tensor_tensor(stat[:, 8 + t:9 + t], stat[:, 4 + t:5 + t], half_pow[:, 0:1], ALU.pow
                                   ).then_inc(rstd_x, 1)
            for b in range(4):
                pool.wait_ge(var_q, b + 1)
                v = sumsq[:, b, :, 0:NORMED[b] // HD]
                pool.tensor_tensor(v, v, half_pow[:, 0:NT * (NORMED[b] // HD)].rearrange(
                    "p (t h) -> p t h", t=NT), ALU.pow).then_inc(rstd_q, 1)

            pool.wait_ge(tables_ready, 1)
            pool.wait_ge(pool_step, 2 + 2 * NP)
            pool.wait_ge(qkt_turned, 13)

            def stage(kind, it, s):
                r = it * 2 + s
                pool.wait_ge(scores_read, it * 16 + 8 * s + 8)
                if kind == "a":
                    pool.tensor_copy(q_st[:, s, :], qta[:, bass.ds(r, 1), :].rearrange("p a n -> p (a n)")
                                     ).then_inc(staged, 1)
                else:
                    pool.tensor_copy(q_st[:, s, :], qtb[:, bass.ds(r - 4, 1), :].rearrange("p a n -> p (a n)")
                                     ).then_inc(staged, 1)
                    pool.tensor_copy(k_st[:, s, :], ktb[:, bass.ds(r - 4, 1), :].rearrange("p a n -> p (a n)")
                                     ).then_inc(staged, 1)
                pool.tensor_copy(slope2[:, :], nslope[:, bass.ds(r * 2, 2)]).then_inc(slope_ready, 1)
                copied = pool.to_reg(r + 1)
                for hh in range(2):
                    pool.wait_ge(tables_ready, 1)
                    if hh == 0:
                        pool.wait_ge(slope_ready, copied)
                    pool.tensor_scalar(table[:, s, hh, :], dist[:, :], slope2[:, hh:hh + 1], None, ALU.mult
                                       ).then_inc(scaled, 1)
                for hh in range(2):
                    pool.wait_ge(scaled, r * 2 + hh + 1)
                    pool.tensor_tensor(table[:, s, hh, :], table[:, s, hh, :], (log_a if kind == "a" else log_b)[:, :],
                                       ALU.add).then_inc(bias_ready, 1)

            pool.wait_ge(qkt_copied[0], 7)
            pool.wait_ge(qkt_copied[1], 6)
            with pool.Fori(0, 2) as it:
                for s in range(2):
                    stage("a", it, s)
            with pool.Fori(2, 4) as it:
                for s in range(2):
                    stage("b", it, s)
            for t in range(NT):
                pool.wait_ge(var_1, t + 1)
                pool.tensor_tensor(stat[:, 8 + t:9 + t], stat[:, 4 + t:5 + t], half_pow[:, 0:1], ALU.pow
                                   ).then_inc(rstd_1, 1)

            def item(i):
                for c in POOL_LO:
                    pool.wait_ge(hi_done, i * CH + c + 1)
                    pool.tensor_tensor(w_lo[:, c % PARTS, :], raw[:, c % RAW, :],
                                       w_hi[:, c % PARTS, :].bitcast(F32), ALU.subtract).then_inc(lo_done[1], 1)

            with pool.Fori(0, NE) as i:
                item(i)
            pool.wait_ge(over_ready, 1)
            n_items = pool.value_load(over_i[0:1, OVER:OVER + 1], min_val=NE, max_val=NE + OVER)
            with pool.If(n_items > NE):
                with pool.Fori(NE, n_items) as i:
                    item(i)

        @block.scalar
        def _(act):
            for t in range(NT):
                act.wait_ge(x_in[t], 16)
                if t >= 1:
                    act.wait_ge(sq_x, t)
                act.activation(xt[:, 0:2, :], acc[:, t, :].rearrange("p (a n) -> p a n", a=2), ACT.Square,
                               accum_out=stat[:, t:t + 1]).then_inc(sq_x, 1)
            for t in range(NT):
                act.wait_ge(xt_turned, 2 * t + 1)
                act.activation(xt[:, 0:4, t * P:(t + 1) * P], bank(2 * t).rearrange("p (k n) -> p k n", k=4),
                               ACT.Copy).then_inc(xt_copied[0], 1)
            n_sq = 0

            def turn_copy(n, dst, col):
                act.wait_ge(head_ready, 1)
                act.wait_ge(qkt_turned, n + 1)
                act.activation(dst, bank(6 + n % 2), ACT.Copy, scale=head_g[:, col:col + 1]
                               ).then_inc(qkt_copied[0], 1)

            pieces = turn_pieces(qta, kta, qtb, ktb)
            for b, (lo, hi) in enumerate(BLOCKS):
                for t in range(NT):
                    g = 4 * b + t
                    act.wait_ge(qkv_done, g + 1)
                    last = act.activation(paired(b, qkv[:, t, lo:hi]), banked(b, bank(g % 6)[:, 0:hi - lo]), ACT.Copy)
                    if b < 4:
                        w = NORMED[b]
                        if n_sq >= 2:
                            act.wait_ge(sq_read, n_sq - 1)
                        last = act.activation(paired(b, squares[:, n_sq % 2, 0:w]), banked(b, bank(g % 6)[:, 0:w]),
                                              ACT.Square)
                        last.then_inc(qkv_copied, 1)
                        n_sq += 1
                    else:
                        last.then_inc(qkv_copied, 1)
                for n, dst, col in pieces[b - 1] if b >= 1 else ():
                    if n % 2 == 0:
                        turn_copy(n, dst, col)
            act.sem_inc(pt_copied[0], 1)

            def exp_unit(kind, it, u):
                i = (u % UN) // 2
                w = (keys(kind, i)[1] - keys(kind, i)[0]) * P
                act.wait_ge(max_ready, it * 16 + u + 1)
                act.activation(probs[:, u % 4, 0:w], probs[:, u % 4, 0:w], ACT.Exp, bias=neg_max[:, u:u + 1],
                               accum_out=den[:, u:u + 1]).then_inc(exp_done, 1)

            def copy_unit(kind, it, u):
                i = (u % UN) // 2
                w = (keys(kind, i)[1] - keys(kind, i)[0]) * P
                act.wait_ge(turned, it * 16 + u + 1 + 4)
                act.activation(probs_t[:, 0, 0:w], bank(4)[:, 0:w], ACT.Copy).then_inc(pt_copied[0], 1)

            def sink_exp(it, s):
                act.wait_ge(sink_d_ready, it * 2 + s + 1)
                act.activation(sink_e[:, 8 * s:8 * s + 8], sink_d[:, 8 * s:8 * s + 8], ACT.Exp
                               ).then_inc(sink_e_ready, 1)

            def attend(kind, it):
                for u in range(16):
                    exp_unit(kind, it, u)
                    if u >= 1 and (u - 1) % 2 == 0:
                        copy_unit(kind, it, u - 1)
                    if kind == "a" and u == 9:
                        sink_exp(it, 0)
                if kind == "a":
                    sink_exp(it, 1)

            with act.Fori(0, 2) as it:
                attend("a", it)
            with act.Fori(2, 4) as it:
                attend("b", it)
            for t in range(NT):
                act.wait_ge(att_turned, 2 * t + 1)
                act.activation(xt[:, 0:4, t * P:(t + 1) * P], bank(2 * t).rearrange("p (k n) -> p k n", k=4),
                               ACT.Copy).then_inc(att_copied[0], 1)
            for t in range(NT):
                act.wait_ge(x1_done, 2 * t + 2)
                if t >= 1:
                    act.wait_ge(sq_1, t)
                act.activation(norm_out[:, :, :], acc[:, t, :].rearrange("p (a n) -> p a n", a=2), ACT.Square,
                               accum_out=stat[:, t:t + 1]).then_inc(sq_1, 1)
            act.wait_ge(bias_in, 64)
            act.wait_ge(hf_ready, NT)
            act.activation(bias_rows[:, :], bias_raw[:, :], ACT.Copy).then_inc(bias_split_hi, 1)
            for t in range(NT):
                act.wait_ge(hf_turned, 2 * t + 1)
                act.activation(xt[:, 0:4, t * P:(t + 1) * P], bank(2 * t).rearrange("p (k n) -> p k n", k=4),
                               ACT.Copy).then_inc(hf_copied[0], 1)
                act.wait_ge(hf_ready, t + 1)
                act.activation(hf_hi[:, t, :], hf[:, t, :], ACT.Copy).then_inc(hf_hi_done, 1)
            act.wait_ge(gap_ready, 1)
            act.activation(top_w[:, :, :], top_w[:, :, :], ACT.Exp).then_inc(gap_exp, 1)
            act.wait_ge(y_zeroed, 1)

            def sel_copy(i):
                act.wait_ge(sel_turned, i + 1)
                act.activation(sel_next[:, :], bank(6), ACT.Copy).then_inc(selt_done, 1)

            def xg_copy(i, q):
                act.wait_ge(gathered, i * 4 + q + 1)
                dst = (x_hi if q < 2 else x_lo)[:, 4 * (q % 2):4 * (q % 2) + 4, :]
                act.activation(dst, bank(7 - q % 2).rearrange("p (k n) -> p k n", k=4), ACT.Copy
                               ).then_inc(xg_done, 1)

            sel_copy(0)
            for q in range(4):
                xg_copy(0, q)

            def part_hi(i, c):
                act.wait_ge(raw_in[c % RAW], i * 32 + 16 * (c // RAW) + 16)
                act.wait_ge(parts_free, i * CH + c + 1)
                act.activation(w_hi[:, c % PARTS, :], raw[:, c % RAW, :], ACT.Copy).then_inc(hi_done, 1)

            def y_high(i):
                act.wait_ge(parts_free, i * CH + 3)
                act.activation(y_hi[:, :], bank(4, 2), ACT.Copy).then_inc(y_hi_done, 1)

            def item(i):
                part_hi(i, 0)
                part_hi(i, 1)
                y_high(i)
                for c in range(2, 10):
                    part_hi(i, c)
                for h in range(2):
                    act.wait_ge(glu_ready, i * 2 + h + 1)
                    act.activation(sig[:, h * 512:(h + 1) * 512], glu[:, h * 512:(h + 1) * 512], ACT.Sigmoid,
                                   scale=ALPHA).then_inc(sig_ready, 1)
                act.wait_ge(sel_turned, i + 2)
                act.wait_ge(selt_done, i + 1)
                act.activation(sel_now[:, :], sel_next[:, :].bitcast(F32), ACT.Copy).then_inc(sel_moved, 1)
                act.wait_ge(sel_moved, i + 1)
                act.activation(sel_next[:, :], bank(6), ACT.Copy).then_inc(selt_done, 1)
                xg_copy(i + 1, 0)
                part_hi(i, 10)
                for q in range(1, 4):
                    xg_copy(i + 1, q)
                for h in range(2):
                    act.wait_ge(act_turned, i * 2 + h + 1)
                    act.activation(act_hi[:, 4 * h:4 * h + 4, :], bank(7 - h).rearrange("p (k n) -> p k n", k=4),
                                   ACT.Copy).then_inc(act_hi_done, 1)
                part_hi(i, 11)

            with act.Fori(0, NE) as i:
                item(i)
            act.wait_ge(over_ready, 1)
            n_items = act.value_load(over_i[0:1, OVER:OVER + 1], min_val=NE, max_val=NE + OVER)
            with act.If(n_items > NE):
                with act.Fori(NE, n_items) as i:
                    item(i)
            y_high(n_items)

        @block.vector
        def _(dve):
            steps = [0]

            def step(ins):
                steps[0] += 1
                ins.then_inc(dve_step, 1)
                dve.wait_ge(dve_step, steps[0])

            for n in range(2):
                dve.wait_ge(gain_rep, n + 1)
                dve.tensor_copy(gain_b[:, n, :], bank(4 + 2 * n, 2)).then_inc(gain_copied, 1)
            for t in range(NT):
                dve.wait_ge(sq_x, t + 1)
                dve.tensor_scalar(stat[:, 4 + t:5 + t], stat[:, t:t + 1], 1.0 / D, EPS, ALU.mult, ALU.add
                                  ).then_inc(var_x, 1)
            dve.wait_ge(gain_copied, 2)
            for t in range(NT):
                dve.wait_ge(rstd_x, t + 1)
                dve.scalar_tensor_tensor(out=xn[:, t, :], in0=acc[:, t, :], scalar=stat[:, 8 + t:9 + t],
                                         in1=gain_b[:, 0, :], op0=ALU.mult, op1=ALU.mult).then_inc(xn_ready, 1)
            for t in range(NT):
                dve.wait_ge(xt_turned, 2 * t + 2)
                dve.tensor_copy(xt[:, 4:8, t * P:(t + 1) * P], bank(2 * t + 1).rearrange("p (k n) -> p k n", k=4)
                                ).then_inc(xt_copied[1], 1)
            dve.wait_ge(head_turned, 1)
            step(dve.tensor_copy(head_g[:, :], bank(0)[:, 0:4]))
            for col in (0, 2):
                last = dve.tensor_scalar(head_g[:, col:col + 1], head_g[:, col:col + 1], HD ** -0.5, None, ALU.mult)
                if col == 0:
                    step(last)
            last.then_inc(head_ready, 1)
            dve.wait_ge(delta_ready, 1)
            step(dve.tensor_copy(tmp_a[:, :], delta_i[:, :]))
            step(dve.scalar_tensor_tensor(out=dist[:, :], in0=tmp_a[:, :], scalar=-1.0, in1=tmp_a[:, :],
                                          op0=ALU.mult, op1=ALU.max))
            step(dve.tensor_scalar(log_a[:, :], dist[:, :], float(A_HALF), NEG, ALU.is_gt, ALU.mult))
            for n, (window, dil) in enumerate(BRANCHES):
                if dil == 1:
                    step(dve.tensor_scalar(tmp_a[:, :], dist[:, :], window / 2.0, None, ALU.is_le))
                    continue
                step(dve.tensor_scalar(low_i[:, :], delta_i[:, :], dil - 1, None, ALU.bitwise_and))
                step(dve.tensor_scalar(tmp_b[:, :], low_i[:, :], 0.0, None, ALU.is_equal))
                step(dve.scalar_tensor_tensor(out=tmp_b[:, :], in0=dist[:, :], scalar=window / 2.0, in1=tmp_b[:, :],
                                              op0=ALU.is_le, op1=ALU.mult))
                step(dve.tensor_tensor(tmp_a[:, :], tmp_a[:, :], tmp_b[:, :], ALU.add))
            step(dve.tensor_scalar(log_b[:, :], tmp_a[:, :], 0.0, NEG, ALU.is_equal, ALU.mult))
            for n, ln in ((2.0, LN2), (3.0, LN3)):
                step(dve.tensor_scalar(tmp_b[:, :], tmp_a[:, :], n, ln, ALU.is_equal, ALU.mult))
                last = dve.tensor_tensor(log_b[:, :], log_b[:, :], tmp_b[:, :], ALU.add)
                if n == 2.0:
                    step(last)
            last.then_inc(tables_ready, 1)

            pieces = turn_pieces(qta, kta, qtb, ktb)
            n_sq = 0
            for b, (lo, hi) in enumerate(BLOCKS):
                if b < 4:
                    w = NORMED[b]
                    nh = w // HD
                    for t in range(NT):
                        dve.wait_ge(qkv_copied, 4 * b + t + 1)
                        last = dve.tensor_reduce(sumsq[:, b, t, 0:nh],
                                                 squares[:, n_sq % 2, 0:w].rearrange("p (h d) -> p h d", d=HD),
                                                 AX.X, ALU.add).then_inc(sq_read, 1)
                        n_sq += 1
                    v = sumsq[:, b, :, 0:nh]
                    dve.wait_ge(sq_read, n_sq)
                    dve.tensor_scalar(v, v, 1.0 / HD, EPS, ALU.mult, ALU.add).then_inc(var_q, 1)
                    dve.wait_ge(rstd_q, b + 1)
                    for t in range(NT):
                        head = qkv[:, t, lo:lo + w].rearrange("p (h d) -> p h d", d=HD)
                        dve.tensor_tensor(head, head, sumsq[:, b, t, 0:nh].unsqueeze(2).to_broadcast([P, nh, HD]),
                                          ALU.mult).then_inc(qk_normed, 1)
                for n, dst, col in pieces[b - 1] if b >= 1 else ():
                    if n % 2 == 1:
                        dve.wait_ge(qkt_turned, n + 1)
                        dve.tensor_scalar(dst, bank(7), head_g[:, col:col + 1], None, ALU.mult
                                          ).then_inc(qkt_copied[1], 1)
            dve.sem_inc(scores_read, 16)
            dve.sem_inc(pt_copied[1], 1)
            dve.sem_inc(o_read, 4)

            def score_unit(kind, it, u):
                s, hh, i = u // UN, u % 2, (u % UN) // 2
                k0, k1 = keys(kind, i)
                w, off = (k1 - k0) * P, (k0 - i) * P + 384
                units = dve.to_reg(it * 16 + u + 1)
                tables = dve.to_reg(it * 4 + 2 * s + hh + 1) if u % UN < 2 else None
                dve.wait_ge(tables_ready, 1)
                if u % UN < 2:
                    dve.wait_ge(bias_ready, tables)
                dve.wait_ge(scored, units)
                dve.wait_ge(turned, units)
                dve.tensor_tensor_reduce(out=probs[:, u % 4, 0:w], in0=bank(u % 4)[:, 0:w],
                                         in1=table[:, s, hh, off:off + w], scale=1.0, scalar=-3e38,
                                         op0=ALU.add, op1=ALU.max, accum_out=maxes[:, u:u + 1]
                                         ).then_inc(scores_read, 1)
                dve.wait_ge(scores_read, it * 16 + u + 1 + 16)
                if kind == "a":
                    dve.tensor_scalar(neg_max[:, u:u + 1], maxes[:, u:u + 1],
                                      sinks[:, bass.ds(it * 2 + (s + 4 * hh), 1)], -1.0, ALU.max, ALU.mult
                                      ).then_inc(max_ready, 1)
                else:
                    dve.tensor_scalar(neg_max[:, u:u + 1], maxes[:, u:u + 1], -1.0, None, ALU.mult
                                      ).then_inc(max_ready, 1)

            def copy_unit(kind, it, u):
                i = (u % UN) // 2
                w = (keys(kind, i)[1] - keys(kind, i)[0]) * P
                dve.wait_ge(turned, it * 16 + u + 1 + 4)
                dve.tensor_copy(probs_t[:, 1, 0:w], bank(5)[:, 0:w]).then_inc(pt_copied[1], 1)

            def sink_gap(it, s):
                dve.wait_ge(max_ready, it * 16 + 8 * s + 8)
                base = sinks[:, bass.ds(it * 2 + s, 5)]
                two = base.rearrange("p n -> p n")[:, 0:5:4].unsqueeze(1).to_broadcast([P, NT, 2])
                dve.tensor_tensor(sink_d[:, 8 * s:8 * s + 8].rearrange("p (i h) -> p i h", h=2),
                                  neg_max[:, 8 * s:8 * s + 8].rearrange("p (i h) -> p i h", h=2), two, ALU.add
                                  ).then_inc(sink_d_ready, 1)

            def normalise(kind, it, s):
                u8 = slice(8 * s, 8 * s + 8)
                dve.wait_ge(exp_done, it * 16 + 8 * s + 8)
                if kind == "a":
                    dve.wait_ge(sink_e_ready, it * 2 + s + 1)
                    dve.tensor_tensor(den[:, u8], den[:, u8], sink_e[:, u8], ALU.add).then_inc(den_ready, 1)
                    dve.wait_ge(den_ready, it * 2 + s + 1)
                dve.reciprocal(recip[:, u8], den[:, u8]).then_inc(recip_ready, 1)
                dve.wait_ge(recip_ready, it * 2 + s + 1)
                dve.wait_ge(pv_done, it * 2 + s + 1)
                for hh in range(2):
                    if kind == "a":
                        col = it * 2 * HD + ((s + 4 * hh) * HD + ATT)
                    else:
                        col = (it - 2) * 4 * HD + ((2 * s + hh) * HD + ATT + AQ * HD)
                    o = bank(6 + s).rearrange("p (i h d) -> p i h d", h=2, d=HD)[:, :, hh, :]
                    r = recip[:, u8].rearrange("p (i h) -> p i h", h=2)[:, :, hh:hh + 1].to_broadcast([P, NT, HD])
                    dve.tensor_tensor(qkv[:, :, bass.ds(col, HD)], o, r, ALU.mult).then_inc(o_read, 1)

            def attend(kind, it):
                for u in range(16):
                    score_unit(kind, it, u)
                    if u >= 1 and (u - 1) % 2 == 1:
                        copy_unit(kind, it, u - 1)
                    if kind == "a" and u % UN == 7:
                        sink_gap(it, u // UN)
                    if u == 12:
                        normalise(kind, it, 0)
                copy_unit(kind, it, 15)
                normalise(kind, it, 1)

            with dve.Fori(0, 2) as it:
                attend("a", it)
            with dve.Fori(2, 4) as it:
                attend("b", it)
            for t in range(NT):
                dve.wait_ge(att_turned, 2 * t + 2)
                dve.tensor_copy(xt[:, 4:8, t * P:(t + 1) * P], bank(2 * t + 1).rearrange("p (k n) -> p k n", k=4)
                                ).then_inc(att_copied[1], 1)

            def norm_token_tile(t):
                dve.wait_ge(sq_1, t + 1)
                dve.tensor_scalar(stat[:, 4 + t:5 + t], stat[:, t:t + 1], 1.0 / D, EPS, ALU.mult, ALU.add
                                  ).then_inc(var_1, 1)
                dve.wait_ge(rstd_1, t + 1)
                dve.scalar_tensor_tensor(out=hf[:, t, :], in0=acc[:, t, :], scalar=stat[:, 8 + t:9 + t],
                                         in1=gain_b[:, 1, :], op0=ALU.mult, op1=ALU.mult).then_inc(hf_ready, 1)

            for t in range(NT):
                for n in range(2):
                    dve.wait_ge(out_done, 2 * t + n + 1)
                    part = acc[:, t, n * 512:(n + 1) * 512]
                    dve.tensor_tensor(part, bank(2 * t + n), part, ALU.add).then_inc(x1_done, 1)
                if t >= 1:
                    norm_token_tile(t - 1)
            norm_token_tile(NT - 1)
            for t in range(NT):
                dve.wait_ge(hf_turned, 2 * t + 2)
                dve.tensor_copy(xt[:, 4:8, t * P:(t + 1) * P], bank(2 * t + 1).rearrange("p (k n) -> p k n", k=4)
                                ).then_inc(hf_copied[1], 1)
                dve.wait_ge(hf_hi_done, t + 1)
                dve.tensor_tensor(hf_lo[:, t, :], hf[:, t, :], hf_hi[:, t, :].bitcast(F32), ALU.subtract
                                  ).then_inc(hf_lo_done, 1)
            for t in range(NT):
                dve.wait_ge(logits_done, t + 1)
                step(dve.tensor_tensor(logits[:, t, :], bank(2 * t)[:, 0:NE], br_b[:, :], ALU.add))
                step(dve.max(top[:, t, :], logits[:, t, :]))
                last = dve.max_index(top_i[:, t, :], top[:, t, :], logits[:, t, :])
            step(last)
            dve.tensor_tensor(top_w[:, :, :], top[:, :, 0:TOPK], top[:, :, 0:1].to_broadcast([P, NT, TOPK]),
                              ALU.subtract).then_inc(gap_ready, 1)
            step(dve.tensor_copy(top_e[:, :, :], top_i[:, :, 0:TOPK]))
            dve.wait_ge(consts_ready, 5)
            flat_e = top_e[:, :, :].rearrange("p t j -> p (t j)").unsqueeze(2).to_broadcast([P, 16, NE])
            step(dve.tensor_tensor(chosen[:, :, :], slot_iota[:, 0:NE].unsqueeze(1).to_broadcast([P, 16, NE]), flat_e,
                                   ALU.is_equal))
            dve.tensor_reduce(mask[:, :, :], chosen[:, :, :].rearrange("p (t j) e -> p t e j", t=NT), AX.X, ALU.add
                              ).then_inc(mask_ready, 1)
            dve.wait_ge(gap_exp, 1)
            step(dve.tensor_reduce(top_s[:, :], top_w[:, :, :], AX.X, ALU.add))
            step(dve.reciprocal(top_r[:, :], top_s[:, :]))
            step(dve.tensor_tensor(top_w[:, :, :], top_w[:, :, :], top_r[:, :].unsqueeze(2).to_broadcast([P, NT, TOPK]),
                                   ALU.mult))
            step(dve.tensor_tensor(weighed[:, :, :], chosen[:, :, :],
                                   top_w[:, :, :].rearrange("p t j -> p (t j)").unsqueeze(2).to_broadcast([P, 16, NE]),
                                   ALU.mult))
            step(dve.memset(gate_t[:, :, :], 0.0))
            step(dve.tensor_reduce(gate_t[:, :, 1:NE + 1], weighed[:, :, :].rearrange("p (t j) e -> p t e j", t=NT),
                                   AX.X, ALU.add))
            step(dve.memset(pos_t[:, :, :], -1.0))
            dve.wait_ge(pos_done, 1)
            step(dve.scalar_tensor_tensor(out=weighed[:, 0:NT, :], in0=bank(1)[:, 0:NT * NE].rearrange(
                "p (t e) -> p t e", t=NT), scalar=1.0, in1=mask[:, :, :], op0=ALU.add, op1=ALU.mult))
            step(dve.tensor_scalar(pos_t[:, :, 0:NE], weighed[:, 0:NT, :], -1.0, None, ALU.add))

            def select(i):
                place = pos_t[:, :, bass.ds(i, 1)] if not isinstance(i, int) else pos_t[:, :, i:i + 1]
                dve.tensor_tensor(sel[:, :, :], slot_iota[:, :].unsqueeze(1).to_broadcast([P, NT, P]),
                                  place.to_broadcast([P, NT, P]), ALU.is_equal).then_inc(sel_ready, 1)

            def select_bias(i):
                e = item_row[:, bass.ds(i, 1)] if not isinstance(i, int) else item_row[:, i:i + 1]
                dve.tensor_tensor(bias_sel[:, :], row_number[:, :].to_broadcast([2 * NE, P]), e.to_broadcast([2 * NE, P]),
                                  ALU.is_equal).then_inc(bias_sel_ready, 1)

            low = slice(NE, 2 * NE)
            dve.wait_ge(bias_split_hi, 1)
            dve.tensor_tensor(bias_rows[low, :], bias_raw[low, :], bias_rows[low, :].bitcast(F32), ALU.subtract
                              ).then_inc(bias_split_lo, 1)
            step(dve.tensor_copy(item_row[0:NE, :], slot_iota[0:NE, 0:GC]))
            step(dve.tensor_scalar(item_row[low, :], slot_iota[low, 0:GC], float(NE), None, ALU.add))
            select_bias(0)
            dve.wait_ge(hf_copied[0], NT)
            dve.wait_ge(logits_done, NT)
            dve.wait_ge(hf_lo_done, NT)
            select(0)
            step(dve.memset(sel_now[:, :].bitcast(F32), 0.0))
            dve.memset(bank(4, 2), 0.0).then_inc(y_zeroed, 1)
            dve.wait_ge(count_done, 1)
            step(dve.tensor_copy(count[:, :], ps[0:NE, 3 * 512:3 * 512 + 1]))
            step(dve.tensor_scalar(more[:, 0:1], count[:, :], float(P), None, ALU.is_gt))
            for n in (2, 3):
                step(dve.scalar_tensor_tensor(out=more[:, 0:1], in0=count[:, :], scalar=float(n * P), in1=more[:, 0:1],
                                              op0=ALU.is_gt, op1=ALU.add))
            dve.sem_inc(more_ready, 1)
            dve.wait_ge(e_turned, 1)
            step(dve.tensor_copy(pos_e[:, :], ps[0:NE, 0:512]))
            step(dve.tensor_copy(gate_e[:, :], ps[0:NE, 512:1024]))
            dve.wait_ge(first_done, 1)
            step(dve.tensor_copy(more[:, 1:2], ps[0:NE, 2 * 512:2 * 512 + 1]))
            step(dve.tensor_tensor(more[:, 2:3], more[:, 0:1], more[:, 1:2], ALU.add))
            v = slot_iota[0:NE, 0:OVER]
            step(dve.tensor_scalar(item_tm[:, :], v, more[:, 2:3], None, ALU.is_lt))
            step(dve.scalar_tensor_tensor(out=item_in[:, :], in0=v, scalar=more[:, 1:2], in1=item_tm[:, :],
                                          op0=ALU.is_ge, op1=ALU.mult))
            step(dve.tensor_scalar(item_tm[:, :], v, more[:, 1:2], 1.0, ALU.subtract, ALU.add))
            step(dve.scalar_tensor_tensor(out=item_sh[:, :], in0=item_tm[:, :], scalar=float(P), in1=item_in[:, :],
                                          op0=ALU.mult, op1=ALU.mult))
            dve.sem_inc(lists_ready, 1)
            dve.wait_ge(over_done, 1)
            step(dve.tensor_copy(pos_t[:, :, NE:NE + OVER], bank(0)[:, 0:NT * OVER].rearrange("p (t v) -> p t v", t=NT)))
            step(dve.tensor_copy(gate_t[:, :, NE + 1:NE + 1 + OVER],
                                 bank(1)[:, 0:NT * OVER].rearrange("p (t v) -> p t v", t=NT)))
            step(dve.tensor_copy(over_f[:, :], ps[0:1, 2 * 512:2 * 512 + OVER + 1]))
            step(dve.tensor_scalar(over_f[:, OVER:OVER + 1], over_f[:, OVER:OVER + 1], float(NE), None, ALU.add))
            step(dve.tensor_copy(item_row[0:NE, NE:NE + OVER], ps[0:NE, 3 * 512:3 * 512 + OVER]))
            step(dve.tensor_scalar(item_row[low, NE:NE + OVER], ps[low, 3 * 512:3 * 512 + OVER], float(NE), None,
                                   ALU.add))
            dve.tensor_copy(over_i[:, :], over_f[:, :]).then_inc(over_ready, 1)
            dve.wait_ge(over_ready, 1)
            dve.sem_inc(lin_ready, 2)
            dve.sem_inc(act_lo_done, 2)

            def part_lo(i, c):
                if c in POOL_LO:
                    return
                dve.wait_ge(hi_done, i * CH + c + 1)
                dve.tensor_tensor(w_lo[:, c % PARTS, :], raw[:, c % RAW, :], w_hi[:, c % PARTS, :].bitcast(F32),
                                  ALU.subtract).then_inc(lo_done[0], 1)

            def y_low(i):
                dve.wait_ge(y_hi_done, i + 1)
                dve.tensor_tensor(y_lo[:, :], bank(4, 2), y_hi[:, :].bitcast(F32), ALU.subtract
                                  ).then_inc(y_lo_done, 1)

            def accumulate(i, k):
                t, n = k // 2, k % 2
                dve.wait_ge(combined, i * 8 + k + 1)
                part = acc[:, t, n * 512:(n + 1) * 512]
                gate = gate_t[:, t, bass.ds(i, 1)]
                dve.scalar_tensor_tensor(out=part, in0=bank(6 + k % 2), scalar=gate, in1=part,
                                         op0=ALU.mult, op1=ALU.add).then_inc(acc_done, 1)

            def item(i):
                part_lo(i, 0)
                part_lo(i, 1)
                y_low(i)
                part_lo(i, 2)
                accumulate(i, 0)
                dve.wait_ge(gathered, i * 4 + 4)
                select(i + 1)
                for c in range(3, W1C):
                    part_lo(i, c)
                    accumulate(i, c - 2)
                part_lo(i, 8)
                accumulate(i, 6)
                accumulate(i, 7)
                dve.wait_ge(parts_free, i * CH + 11)
                for h in range(2):
                    dve.tensor_scalar(glu[:, h * 512:(h + 1) * 512], bank(h), LIMIT, None, ALU.min
                                      ).then_inc(glu_ready, 1)
                for h in range(2):
                    last = dve.tensor_scalar(lin[:, h * 512:(h + 1) * 512], bank(2 + h), LIMIT, -LIMIT, ALU.min,
                                             ALU.max).then_inc(lin_ready, 1)
                for h in range(2):
                    cols = slice(h * 512, (h + 1) * 512)
                    dve.wait_ge(lin_ready, i * 2 + h + 3)
                    dve.wait_ge(glu_ready, i * 2 + h + 1)
                    dve.scalar_tensor_tensor(out=lin[:, cols], in0=lin[:, cols], scalar=1.0, in1=glu[:, cols],
                                             op0=ALU.add, op1=ALU.mult).then_inc(prod_ready, 1)
                    dve.wait_ge(prod_ready, i * 2 + h + 1)
                    dve.wait_ge(sig_ready, i * 2 + h + 1)
                    dve.tensor_tensor(glu[:, cols], lin[:, cols], sig[:, cols], ALU.mult).then_inc(act_ready, 1)
                part_lo(i, 9)
                for h in range(2):
                    if h:
                        part_lo(i, 10)
                    dve.wait_ge(act_hi_done, i * 2 + h + 1)
                    dve.tensor_tensor(act_lo[:, 4 * h:4 * h + 4, :], bank(7 - h).rearrange("p (k n) -> p k n", k=4),
                                      act_hi[:, 4 * h:4 * h + 4, :].bitcast(F32), ALU.subtract
                                      ).then_inc(act_lo_done, 1)
                part_lo(i, 11)
                dve.wait_ge(bias_used, i + 1)
                select_bias(i + 1)

            with dve.Fori(0, NE) as i:
                item(i)
            dve.wait_ge(over_ready, 1)
            n_items = dve.value_load(over_i[0:1, OVER:OVER + 1], min_val=NE, max_val=NE + OVER)
            with dve.If(n_items > NE):
                with dve.Fori(NE, n_items) as i:
                    item(i)
            y_low(n_items)
            for k in range(8):
                accumulate(n_items, k)

        @block.tensor
        def _(pe):
            pe.wait_ge(rows_in, 32)
            pe.wait_ge(ident_ready, 3)
            for n in range(2):
                for h in range(2):
                    last = pe.matmul(bank(4 + 2 * n + h), ones[0:1, :], rows[0:1, n, h * 512:(h + 1) * 512],
                                     start=True, stop=True)
                last.then_inc(gain_rep, 1)
            for t in range(NT):
                pe.wait_ge(xn_ready, t + 1)
                if t >= 2:
                    pe.wait_ge(gain_copied, t - 1)
                for h in range(2):
                    for k in range(4):
                        last = pe.transpose(bank(2 * t + h)[:, k * P:(k + 1) * P],
                                            xn[:, t, (4 * h + k) * P:(4 * h + k + 1) * P], ident[:, :])
                    last.then_inc(xt_turned, 1)
            pe.wait_ge(small_in, 160)
            pe.wait_ge(xt_copied[0], 1)
            pe.transpose(bank(0)[:, 0:4], gain_rows[:, :], ident[0:4, 0:4]).then_inc(head_turned, 1)
            pe.wait_ge(head_ready, 1)

            def turn_block(b):
                pe.wait_ge(qk_normed, 4 * (b + 1))
                for n, _dst, _col in turn_pieces(qta, kta, qtb, ktb)[b]:
                    j = n - turn_pieces(qta, kta, qtb, ktb)[b][0][0]
                    if n >= 2:
                        pe.wait_ge(qkt_copied[n % 2], n // 2)
                    for t in range(NT):
                        c = BLOCKS[b][0] + j * P
                        last = pe.transpose(bank(6 + n % 2)[:, t * P:(t + 1) * P], qkv[:, t, c:c + P], ident[:, :])
                    last.then_inc(qkt_turned, 1)

            for b, (lo, hi) in enumerate(BLOCKS):
                pe.wait_ge(win_in[b % 3], 16 * (b // 3 + 1))
                w = win_sb(b)
                for t in range(NT):
                    g = 4 * b + t
                    if b == 0:
                        pe.wait_ge(xt_copied[0], t + 1)
                        pe.wait_ge(xt_copied[1], t + 1)
                    if g >= 6:
                        pe.wait_ge(qkv_copied, g - 5)
                    for k in range(ND):
                        last = pe.matmul(bank(g % 6)[:, 0:hi - lo], xt[:, k, t * P:(t + 1) * P], w[:, k, :],
                                         start=(k == 0), stop=(k == ND - 1))
                    last.then_inc(qkv_done, 1)
                pe.wait_ge(qkv_done, 4 * (b + 1))
                pe.sem_inc(win_used, 1)
                if b >= 1:
                    turn_block(b - 1)

            pe.sem_inc(turned, 4)
            pe.wait_ge(qkv_copied, 20)

            def score(kind, it, u):
                s, hh, i = u // UN, u % 2, (u % UN) // 2
                k0, k1 = keys(kind, i)
                if u % UN == 0:
                    pe.wait_ge(staged, (it * 2 + s + 1) if kind == "a" else (it * 4 + 2 * s - 2))
                pe.wait_ge(scores_read, it * 16 + u + 13)
                kt = kta[:, :] if kind == "a" else k_st[:, s, :]
                pe.matmul(bank(u % 4)[:, 0:(k1 - k0) * P], q_st[hh * HD:(hh + 1) * HD, s, i * P:(i + 1) * P],
                          kt[hh * HD:(hh + 1) * HD, k0 * P:k1 * P], start=True, stop=True).then_inc(scored, 1)

            def turn(kind, it, u):
                i = (u % UN) // 2
                k0, k1 = keys(kind, i)
                pe.wait_ge(exp_done, it * 16 + u + 1)
                pe.wait_ge(pt_copied[u % 2], it * 8 + u // 2 + 1)
                for k in range(k1 - k0):
                    last = pe.transpose(bank(4 + u % 2)[:, k * P:(k + 1) * P], probs[:, u % 4, k * P:(k + 1) * P],
                                        ident[:, :])
                last.then_inc(turned, 1)

            def values(kind, it, u):
                s, hh, i = u // UN, u % 2, (u % UN) // 2
                k0, k1 = keys(kind, i)
                pe.wait_ge(pt_copied[u % 2], it * 8 + u // 2 + 2)
                if u % UN == 0:
                    pe.wait_ge(o_read, it * 4 + 2 * s + 2)
                for k in range(k0, k1):
                    if kind == "a":
                        v = qkv[:, k, VA + hh * HD:VA + (hh + 1) * HD]
                    else:
                        v = qkv[:, k, bass.ds((it - 2) * 4 * HD + ((2 * s + hh) * HD + VB), HD)]
                    last = pe.matmul(bank(6 + s)[:, (u % UN) * HD:(u % UN + 1) * HD],
                                     probs_t[:, u % 2, (k - k0) * P:(k - k0 + 1) * P], v,
                                     start=(k == k0), stop=(k == k1 - 1))
                if u % UN == UN - 1:
                    last.then_inc(pv_done, 1)

            def attend(kind, it):
                score(kind, it, 0)
                score(kind, it, 1)
                for u in range(16):
                    if u + 2 < 16:
                        score(kind, it, u + 2)
                    turn(kind, it, u)
                    if u >= 1:
                        values(kind, it, u - 1)
                values(kind, it, 15)

            with pe.Fori(0, 2) as it:
                attend("a", it)
            with pe.Fori(2, 4) as it:
                attend("b", it)

            pe.wait_ge(o_read, 2 * NP + 4)
            pe.wait_ge(scores_read, NP * UN + 16)
            for p in range(2):
                pe.wait_ge(pt_copied[p], NP * UN // 2 + 1)
            for t in range(NT):
                for h in range(2):
                    for k in range(4):
                        c = ATT + (4 * h + k) * P
                        last = pe.transpose(bank(2 * t + h)[:, k * P:(k + 1) * P], qkv[:, t, c:c + P], ident[:, :])
                    last.then_inc(att_turned, 1)
            pe.wait_ge(wout_in, 16)
            for t in range(NT):
                pe.wait_ge(att_copied[0], t + 1)
                pe.wait_ge(att_copied[1], t + 1)
                for n in range(2):
                    for k in range(ND):
                        last = pe.matmul(bank(2 * t + n), xt[:, k, t * P:(t + 1) * P],
                                         wout_sb[:, k, n * 512:(n + 1) * 512], start=(k == 0), stop=(k == ND - 1))
                    last.then_inc(out_done, 1)
            pe.wait_ge(router_in, 16)
            for t in range(NT):
                pe.wait_ge(hf_ready, t + 1)
                pe.wait_ge(x1_done, 2 * t + 2)
                pe.wait_ge(out_done, 2 * NT)
                for h in range(2):
                    for k in range(4):
                        last = pe.transpose(bank(2 * t + h)[:, k * P:(k + 1) * P],
                                            hf[:, t, (4 * h + k) * P:(4 * h + k + 1) * P], ident[:, :])
                    last.then_inc(hf_turned, 1)
            for t in range(NT):
                pe.wait_ge(hf_copied[0], t + 1)
                pe.wait_ge(hf_copied[1], t + 1)
                for k in range(ND):
                    last = pe.matmul(bank(2 * t)[:, 0:NE], xt[:, k, t * P:(t + 1) * P], wr[:, k, :],
                                     start=(k == 0), stop=(k == ND - 1))
                last.then_inc(logits_done, 1)
            pe.wait_ge(mask_ready, 1)
            for t in range(NT):
                for s in range(t + 1):
                    last = pe.matmul(bank(1)[:, t * NE:(t + 1) * NE], (before if s == t else ones)[:, :], mask[:, s, :],
                                     start=(s == 0), stop=(s == t))
            last.then_inc(pos_done, 1)
            for t in range(NT):
                last = pe.matmul(ps[0:NE, 3 * 512:3 * 512 + 1], mask[:, t, :], ones[:, 0:1],
                                 start=(t == 0), stop=(t == NT - 1))
            last.then_inc(count_done, 1)
            pe.sem_inc(parts_free, PARTS)

            def turn_selection():
                for t in range(NT):
                    last = pe.transpose(bank(6)[:, t * P:(t + 1) * P], sel[:, t, :].bitcast(F32), ident[:, :])
                last.then_inc(sel_turned, 1)

            def gather(q):
                src = hf_hi if q < 2 else hf_lo
                for k in range(4):
                    d = 4 * (q % 2) + k
                    for t in range(NT):
                        last = pe.matmul(bank(7 - q % 2)[:, k * P:(k + 1) * P], src[:, t, d * P:(d + 1) * P],
                                         sel[:, t, :], start=(t == 0), stop=(t == NT - 1))
                last.then_inc(gathered, 1)

            pe.wait_ge(sel_ready, 1)
            turn_selection()
            for q in range(4):
                if q == 1:
                    pe.wait_ge(selt_done, 1)
                if q >= 2:
                    pe.wait_ge(xg_done, q - 1)
                gather(q)
            pe.wait_ge(more_ready, 1)
            for j, src in ((0, pos_t[:, :, 0:NE]), (1, gate_t[:, :, 1:NE + 1])):
                for t in range(NT):
                    last = pe.transpose(ps[0:NE, j * 512 + t * P:j * 512 + (t + 1) * P], src[:, t, :], ident[:, :])
            last.then_inc(e_turned, 1)
            pe.matmul(ps[0:NE, 2 * 512:2 * 512 + 1], before[0:NE, 0:NE], more[:, 0:1], start=True, stop=True
                      ).then_inc(first_done, 1)
            pe.wait_ge(lists_ready, 1)
            for t in range(NT):
                o = bank(0)[:, t * OVER:(t + 1) * OVER]
                pe.matmul(o, pos_e[:, t * P:(t + 1) * P], item_in[:, :], start=True, stop=False)
                pe.matmul(o, neg_ones[:, :], item_sh[:, :], start=False, stop=True)
                pe.matmul(bank(1)[:, t * OVER:(t + 1) * OVER], gate_e[:, t * P:(t + 1) * P], item_in[:, :],
                          start=True, stop=True)
            pe.matmul(ps[0:1, 2 * 512:2 * 512 + OVER], e_iota[:, :], item_in[:, :], start=True, stop=True)
            pe.matmul(ps[0:1, 2 * 512 + OVER:2 * 512 + OVER + 1], ones[0:NE, 0:1], more[:, 0:1], start=True, stop=True
                      )
            pe.matmul(ps[0:2 * NE, 3 * 512:3 * 512 + OVER], e_iota[:, :].to_broadcast([NE, 2 * NE]), item_in[:, :],
                      start=True, stop=True).then_inc(over_done, 1)
            pe.wait_ge(bias_split_lo, 1)

            def part_ready(i, c):
                pool = c in POOL_LO
                n = len(POOL_LO) if pool else CH - len(POOL_LO)
                pe.wait_ge(lo_done[pool], i * n + lo_before(c, pool))

            def combine(i, k):
                t, n = k // 2, k % 2
                if k == 0:
                    pe.wait_ge(y_lo_done, i + 1)
                    pe.wait_ge(selt_done, i + 1)
                if k < 2:
                    pe.wait_ge(act_lo_done, i * 2 + 2)
                else:
                    pe.wait_ge(acc_done, i * 8 + k - 1)
                cols = slice(n * 512, (n + 1) * 512)
                pe.matmul(bank(6 + k % 2), sel_now[:, t * P:(t + 1) * P], y_hi[:, cols], start=True, stop=False)
                pe.matmul(bank(6 + k % 2), sel_now[:, t * P:(t + 1) * P], y_lo[:, cols], start=False, stop=True
                          ).then_inc(combined, 1)

            def item(i):
                pe.wait_ge(bias_sel_ready, i + 1)
                pe.wait_ge(lin_ready, i * 2 + 2)
                pe.wait_ge(xg_done, i * 4 + 4)
                for c in range(4):
                    pe.matmul(bank(c), bias_sel[:, :], bias_rows[:, c * 512:(c + 1) * 512], start=True, stop=False)
                for k in range(W1C):
                    part_ready(i, k)
                    s = k % PARTS
                    for lhs, rhs in ((x_hi, w_hi), (x_hi, w_lo), (x_lo, w_hi)):
                        for c in range(4):
                            last = pe.matmul(bank(c), lhs[:, k, :], rhs[:, s, c * 512:(c + 1) * 512],
                                             start=False, stop=(k == W1C - 1 and lhs is x_lo))
                    last.then_inc(parts_free, 1)
                    combine(i, k)
                pe.wait_ge(sel_ready, i + 2)
                pe.wait_ge(acc_done, i * 8 + 7)
                turn_selection()
                for q in range(4):
                    if q == 0:
                        pe.wait_ge(acc_done, i * 8 + 8)
                    elif q == 1:
                        pe.wait_ge(selt_done, i + 2)
                    else:
                        pe.wait_ge(xg_done, i * 4 + 4 + q - 1)
                    gather(q)
                for h in range(2):
                    pe.wait_ge(act_ready, i * 2 + h + 1)
                    pe.wait_ge(xg_done, i * 4 + 4 + 3 + h)
                    for k in range(4):
                        f = 4 * h + k
                        last = pe.transpose(bank(7 - h)[:, k * P:(k + 1) * P], glu[:, f * P:(f + 1) * P], ident[:, :])
                    last.then_inc(act_turned, 1)
                for n in range(2):
                    last = pe.matmul(bank(4 + n), bias_sel[:, :], bias_rows[:, 2048 + n * 512:2048 + (n + 1) * 512],
                                     start=True, stop=False)
                last.then_inc(bias_used, 1)
                for c in range(W1C, CH):
                    if c == W1C:
                        pe.wait_ge(act_lo_done, i * 2 + 3)
                    if c == W1C + 2:
                        pe.wait_ge(act_lo_done, i * 2 + 4)
                    part_ready(i, c)
                    s = c % PARTS
                    for j in range(2):
                        f = 2 * (c - W1C) + j
                        for lhs, rhs in ((act_hi, w_hi), (act_hi, w_lo), (act_lo, w_hi)):
                            for n in range(2):
                                last = pe.matmul(bank(4 + n), lhs[:, f, :],
                                                 rhs[:, s, j * 1024 + n * 512:j * 1024 + (n + 1) * 512],
                                                 start=False, stop=(c == CH - 1 and j == 1 and lhs is act_lo))
                    last.then_inc(parts_free, 1)

            with pe.Fori(0, NE) as i:
                item(i)
            pe.wait_ge(over_ready, 1)
            n_items = pe.value_load(over_i[0:1, OVER:OVER + 1], min_val=NE, max_val=NE + OVER)
            with pe.If(n_items > NE):
                with pe.Fori(NE, n_items) as i:
                    item(i)
            for k in range(8):
                combine(n_items, k)


def turn_pieces(qta, kta, qtb, ktb):
    return (
        [(j, qta[:, j, :], 0) for j in range(4)],
        [(4, kta[:, :], 1)],
        [(5 + j, qtb[:, j, :], 2) for j in range(4)],
        [(9 + j, ktb[:, j, :], 3) for j in range(4)],
    )


_INS = ["x", "attn_norm_g", "w_in", "a_q_norm_g", "a_k_norm_g", "a_sinks", "b_q_norm_g", "b_k_norm_g",
        "w_out", "ffn_norm_g", "w_router", "b_router", "w1", "b1", "w2", "b2"]


def kernel(**inputs):
    import numpy as np
    import concourse.bacc as bacc
    from concourse.bass_utils import run_bass_kernel_spmd

    nc = bacc.Bacc("TRN2", target_bir_lowering=False, num_devices=1, dynamic_dma_scratch_size=64)
    arrays, args = {}, []
    for name in _INS:
        a = np.ascontiguousarray(inputs[name])
        arrays[f"in_{name}"] = a
        args.append(nc.dram_tensor(f"in_{name}", a.shape, mybir.dt.from_np(a.dtype), kind="ExternalInput").ap())
    out = nc.dram_tensor("out", (1, SEQ, D), F32, kind="ExternalOutput").ap()
    layer(nc, *args, out)
    r = run_bass_kernel_spmd(nc, [arrays], core_ids=[0])
    return r.results[0]["out"]
```

```python
from contextlib import ExitStack

import concourse.bass as bass
from concourse import mybir

F32 = mybir.dt.float32
F32R = mybir.dt.float32r
I32 = mybir.dt.int32
U32 = mybir.dt.uint32
ALU = mybir.AluOpType
ACT = mybir.ActivationFunctionType
AX = mybir.AxisListType

P = 128
SEQ = 512
D = 1024
NT = SEQ // P
ND = D // P
HD = 64
AQ, AKV, BH = 8, 2, 8
NE, TOPK, FF = 32, 4, 1024
EPS = 1e-5
LIMIT, ALPHA = 7.0, 1.702
NEG = -1e30
A_HALF = 128
BRANCHES = ((128, 1), (512, 4), (2048, 16))
LN2, LN3 = 0.6931471805599453, 1.0986122886681098

BLOCKS = ((512, 768), (0, 512), (768, 1280), (1280, 1792), (1792, 2304))
NORMED = (128, 512, 512, 512)
PROJ_W = 2304
VA, VB, ATT = 640, 1792, 768

NP = 8
UN = 8
LEAD = 3
CH = 12
W1C = 8
RING = 6
POOL_LO = (1, 4, 7, 10)
OVER = 16
GC = NE + OVER + 3
KB = 1024


def number(i, c):
    return i * CH + (c - 4)


def slot(c):
    return (c + 2) % RING


def split_count(i, c, pool):
    mine = [k for k in range(CH) if (k in POOL_LO) == pool]
    return i * len(mine) + (sum(k <= c for k in mine) - sum(k < 4 for k in mine))


def layer(nc, x, attn_norm_g, w_in, a_q_norm_g, a_k_norm_g, a_sinks, b_q_norm_g, b_k_norm_g,
          w_out, ffn_norm_g, w_router, b_router, w1, b1, w2, b2, out):
    ctx = ExitStack()
    with ctx:
        def at(name, shape, dt, offset):
            return nc.alloc_sbuf_tensor_at(name, shape, dt, offset=64 + offset)

        acc = at("acc", [P, NT, D], F32, 0)
        raw = at("raw", [P, RING, 2048], F32, 16 * KB)
        w_lo = at("w_lo", [P, RING, 2048], F32R, 16 * KB)
        c0 = 64 * KB
        ident = at("ident", [P, P], F32, c0)
        slot_iota = at("slot_iota", [P, P], F32, c0 + 512)
        ones = at("ones", [P, P], F32, c0 + 1024)
        before = at("before", [P, P], F32, c0 + 1536)
        wr = at("wr", [P, ND, NE], F32, c0 + 2048)
        gate_t = at("gate_t", [P, NT, GC], F32, c0 + 3072)
        pos_t = at("pos_t", [P, NT, GC], F32, c0 + 3904)
        c1 = c0 + 4736
        br_b = at("br_b", [P, NE], F32, c1)
        sinks = at("sinks", [P, AQ], F32, c1 + 128)
        head_g = at("head_g", [P, 4], F32, c1 + 224)
        half_pow = at("half_pow", [P, P], F32, c1 + 256)
        stat = at("stat", [P, 16], F32, c1 + 768)
        bias_sel = at("bias_sel", [2 * NE, P], F32R, c1 + 832)
        row_number = at("row_number", [2 * NE, 1], F32, c1 + 1440)
        item_row = at("item_row", [2 * NE, GC], F32, c1 + 1472)
        items = at("items", [1, GC], I32, c1 + 1696)

        r1 = 71 * KB
        qkv = at("qkv", [P, NT, PROJ_W], F32, r1)
        qta = at("qta", [P, 4, SEQ], F32, r1 + 36864)
        kta = at("kta", [P, SEQ], F32, r1 + 45056)
        qtb = at("qtb", [P, 4, SEQ], F32, r1 + 47104)
        ktb = at("ktb", [P, 4, SEQ], F32, r1 + 55296)
        dist = at("dist", [P, 896], F32, r1 + 63488)
        logs = at("logs", [P, 2, 896], F32, r1 + 67072)
        table = at("table", [P, 2, 2, 896], F32, r1 + 74240)
        delta_i = at("delta_i", [P, 896], I32, r1 + 74240)
        low_i = at("low_i", [P, 896], I32, r1 + 74240 + 3584)
        tmp_a = at("tmp_a", [P, 896], F32, r1 + 74240 + 7168)
        tmp_b = at("tmp_b", [P, 896], F32, r1 + 74240 + 10752)
        sumsq = at("sumsq", [P, 4, NT, 8], F32, r1 + 88576)
        maxes = at("maxes", [P, 16], F32, r1 + 89088)
        neg_max = at("neg_max", [P, 16], F32, r1 + 89152)
        den = at("den", [P, 16], F32, r1 + 89216)
        sink_d = at("sink_d", [P, 16], F32, r1 + 89280)
        sink_e = at("sink_e", [P, 16], F32, r1 + 89344)
        recip = at("recip", [P, 16], F32, r1 + 89408)
        nslope = at("nslope", [P, 2 * NP + 2], F32, r1 + 90016)
        gain_rows = at("gain_rows", [4, P], F32, r1 + 89504)
        att_lo = at("att_lo", [P, ND, SEQ], F32R, r1 + 40960)
        wout_hi_last = at("wout_hi_last", [P, 2, 2048], F32R, r1 + 90 * KB + 40960)
        norm_out = at("norm_out", [P, 2, 512], F32, r1 + 36864)
        bias_raw = at("bias_raw", [2 * NE, 2048], F32, r1 + 57344)
        hf_hi = at("hf_hi", [P, NT, D], F32R, r1)
        hf_lo = at("hf_lo", [P, NT, D], F32R, r1 + 16384)
        w_hi = at("w_hi", [P, RING, 2048], F32R, r1 + 32768)
        y_hi = at("y_hi", [P, D], F32R, r1 + 81920)
        y_lo = at("y_lo", [P, D], F32R, r1 + 86016)

        r2 = r1 + 90 * KB
        xn = at("xn", [P, NT, D], F32, r2)
        xt = at("xt", [P, ND, SEQ], F32, r2 + 16384)
        gain_b = at("gain_b", [P, 2, D], F32, r2 + 32768)
        win_hi = at("win_hi", [P, 2, 2048], F32R, r2)
        win_hi_first = at("win_hi_first", [P, 2, 2048], F32R, r1 + 47104)
        squares = at("squares", [P, 2, 512], F32, r2 + 59840)
        xt_hi = at("xt_hi", [P, ND, SEQ], F32R, r2 + 16384)
        xt_lo = at("xt_lo", [P, ND, SEQ], F32R, r2 + 40960)
        probs = at("probs", [P, 4, 512], F32, r2)
        probs_t = at("probs_t", [P, 2, 512], F32, r2 + 8192)
        q_st = at("q_st", [P, 2, SEQ], F32, r2 + 32768)
        k_st = at("k_st", [P, 2, SEQ], F32, r2 + 16384)
        hf = at("hf", [P, NT, D], F32, r2)
        rows = at("rows", [1, 2, D], F32, r1)
        x_hi = at("x_hi", [P, ND, P], F32R, r2)
        x_lo = at("x_lo", [P, ND, P], F32R, r2 + 4096)
        glu = at("glu", [P, FF], F32, r2 + 8192)
        lin = at("lin", [P, FF], F32, r2 + 12288)
        sig = at("sig", [P, FF], F32, r2 + 16384)
        act_hi = at("act_hi", [P, ND, P], F32R, r2 + 20480)
        act_lo = at("act_lo", [P, ND, P], F32R, r2 + 24576)
        sel = at("sel", [P, NT, P], F32R, r2 + 28672)
        sel_c = at("sel_c", [P, NT, P], F32R, r2 + 30720)
        sel_t = at("sel_t", [P, SEQ], F32R, r2 + 32768)
        bias_rows = at("bias_rows", [2 * NE, 2048], F32R, r2 + 34816)
        b2_rows = at("b2_rows", [NE, D], F32, r2 + 43008)
        r3 = r2 + 49152
        chosen = at("chosen", [P, 16, NE], F32, r3)
        weighed = at("weighed", [P, 16, NE], F32, r3 + 2048)
        logits = at("logits", [P, NT, NE], F32, r3 + 10688)
        mask = at("mask", [P, NT, NE], F32, r3 + 11200)
        top = at("top", [P, NT, 8], F32, r3 + 11712)
        top_i = at("top_i", [P, NT, 8], U32, r3 + 11840)
        top_e = at("top_e", [P, NT, TOPK], F32, r3 + 11968)
        top_w = at("top_w", [P, NT, TOPK], F32, r3 + 12032)
        top_s = at("top_s", [P, NT], F32, r3 + 12096)
        top_r = at("top_r", [P, NT], F32, r3 + 12128)
        pos_e = at("pos_e", [NE, SEQ], F32, r3 + 5568)
        gate_e = at("gate_e", [NE, SEQ], F32, r3 + 7616)
        r4 = r3 + 9664
        count = at("count", [NE, 1], F32, r4)
        more = at("more", [NE, 4], F32, r4 + 32)
        item_in = at("item_in", [NE, OVER], F32, r4 + 64)
        item_sh = at("item_sh", [NE, OVER], F32, r4 + 128)
        item_tm = at("item_tm", [NE, OVER], F32, r4 + 192)
        e_iota = at("e_iota", [NE, 1], F32, r4 + 256)
        neg_ones = at("neg_ones", [NE, P], F32, r4 + 288)
        item_f = at("item_f", [1, GC], F32, r4 + 800)
        x_tok = at("x_tok", [P, D], F32, r4 + 1024)

        ps = ctx.enter_context(nc.psum_tensor("ps", [P, 8 * 512], F32))

        def bank(b, n=1):
            return ps[:, b * 512:(b + n) * 512]

        def sem(name):
            return ctx.enter_context(nc.semaphore(name))

        x_in = [sem(f"x_in{t}") for t in range(NT)]
        rows_in, small_in, router_in = sem("rows_in"), sem("small_in"), sem("router_in")
        win_in = [sem(f"win_in{s}") for s in range(RING)]
        bias_in, b2_in, wout_in, out_stored = sem("bias_in"), sem("b2_in"), sem("wout_in"), sem("out_stored")
        b2_spread, b2_added = sem("b2_spread"), sem("b2_added")
        raw_in = [sem(f"raw_in{s}") for s in range(RING)]

        ident_ready, consts_ready, pool_step = sem("ident_ready"), sem("consts_ready"), sem("pool_step")
        dve_step = sem("dve_step")
        bias_split_hi, bias_split_lo = sem("bias_split_hi"), sem("bias_split_lo")
        gain_rep, gain_copied = sem("gain_rep"), sem("gain_copied")
        sq_x, var_x, rstd_x, xn_ready = sem("sq_x"), sem("var_x"), sem("rstd_x"), sem("xn_ready")
        xt_turned = sem("xt_turned")
        xt_copied = [sem("xt_copied_act"), sem("xt_copied_dve")]
        head_turned, head_ready = sem("head_turned"), sem("head_ready")
        win_hi_done, win_lo_done = sem("win_hi_done"), sem("win_lo_done")
        half_used, qkv_done, qkv_copied = sem("half_used"), sem("qkv_done"), sem("qkv_copied")
        sq_read = sem("sq_read")
        var_q, rstd_q, qk_normed = sem("var_q"), sem("rstd_q"), sem("qk_normed")
        qkt_turned = sem("qkt_turned")
        qkt_copied = [sem("qkt_copied_act"), sem("qkt_copied_dve")]
        delta_ready, tables_ready = sem("delta_ready"), sem("tables_ready")
        staged, bias_ready = sem("staged"), sem("bias_ready")
        scored, scores_read, max_ready, exp_done = sem("scored"), sem("scores_read"), sem("max_ready"), sem("exp_done")
        turned, pv_done, o_read = sem("turned"), sem("pv_done"), sem("o_read")
        pt_copied = [sem("pt_copied_act"), sem("pt_copied_dve")]
        sink_d_ready, sink_e_ready, den_ready, recip_ready = (
            sem("sink_d_ready"), sem("sink_e_ready"), sem("den_ready"), sem("recip_ready"))
        att_turned, wout_hi_done, wout_lo_done = sem("att_turned"), sem("wout_hi_done"), sem("wout_lo_done")
        att_copied = [sem("att_copied_act"), sem("att_copied_dve")]
        out_done, x1_done = sem("out_done"), sem("x1_done")
        sq_1, var_1, rstd_1, hf_ready = sem("sq_1"), sem("var_1"), sem("rstd_1"), sem("hf_ready")
        hf_hi_done, hf_lo_done, hf_turned = sem("hf_hi_done"), sem("hf_lo_done"), sem("hf_turned")
        hf_copied = [sem("hf_copied_act"), sem("hf_copied_dve")]
        logits_done = sem("logits_done")
        gap_ready, gap_exp = sem("gap_ready"), sem("gap_exp")
        mask_ready, pos_done, count_done = sem("mask_ready"), sem("pos_done"), sem("count_done")
        e_turned = sem("e_turned")
        more_ready, first_done, lists_ready = sem("more_ready"), sem("first_done"), sem("lists_ready")
        over_done, items_ready = sem("over_done"), sem("items_ready")

        hi_done, chunk_used = sem("hi_done"), sem("chunk_used")
        lo_done = [sem("lo_done_dve"), sem("lo_done_pool")]
        bias_sel_ready, bias_used = sem("bias_sel_ready"), sem("bias_used")
        glu_ready, lin_ready, sig_ready = sem("glu_ready"), sem("lin_ready"), sem("sig_ready")
        prod_ready, act_ready = sem("prod_ready"), sem("act_ready")
        act_turned, act_hi_done, act_lo_done = sem("act_turned"), sem("act_hi_done"), sem("act_lo_done")
        y_zeroed, y_hi_done, y_lo_done = sem("y_zeroed"), sem("y_hi_done"), sem("y_lo_done")
        sel_ready, sel_c_ready, sel_turned, sel_t_done = (
            sem("sel_ready"), sem("sel_c_ready"), sem("sel_turned"), sem("sel_t_done"))
        gathered, x_tok_done, x_turned = sem("gathered"), sem("x_tok_done"), sem("x_turned")
        x_hi_done, x_lo_done = sem("x_hi_done"), sem("x_lo_done")
        combined, acc_done = sem("combined"), sem("acc_done")

        block = ctx.enter_context(nc.Block())

        win_v = w_in[0].rearrange("(k p) n -> p k n", p=P)

        def half(ring, m, places):
            w = BLOCKS[m // 2][1] - BLOCKS[m // 2][0]
            return ring[:, m % places, 0:4 * w].rearrange("p (k n) -> p k n", k=4)

        def win_high_of(m):
            return half(win_hi_first if m < 4 else win_hi, m, 2)

        def wait_half_used(engine, m):
            if m % 2 == 0:
                engine.wait_ge(half_used, m // 2 + 1)
            else:
                engine.wait_ge(qkv_done, NT * (m // 2 + 1))

        wout_sb = raw[:, 2:6, :].rearrange("p s n -> p (s n)").rearrange("p (k n) -> p k n", k=ND)

        def wout_hi(c):
            return w_lo[:, c, :] if c < 2 else wout_hi_last[:, c - 2, :]

        def wout_split(it, j):
            hi = (wout_hi_last if j else w_lo)[:, bass.ds(it - 2, 1), :]
            return (ap.rearrange("p a n -> p (a n)") for ap in
                    (hi, raw[:, bass.ds(it + 2 * j, 1), :], w_lo[:, bass.ds(it + 2 * j, 1), :]))


        def paired(b, ap):
            return ap.rearrange("p (j g d) -> p g j d", g=2, d=HD) if b == 1 else ap

        def banked(b, ap):
            return ap.rearrange("p (g j d) -> p g j d", g=2, d=HD) if b == 1 else ap

        def keys(kind, i):
            return (max(0, i - 1), min(NT, i + 2)) if kind == "a" else (0, NT)

        @block.sync
        def _(sp):
            for t in range(NT):
                sp.dma_start(acc[:, t, :], x[0, t * P:(t + 1) * P, :]).then_inc(x_in[t], 16)
            sp.dma_start(rows[:, 0, :], attn_norm_g).then_inc(rows_in, 16)
            sp.dma_start(rows[:, 1, :], ffn_norm_g).then_inc(rows_in, 16)

            def load_win(m):
                lo, hi = BLOCKS[m // 2]
                k = 4 * (m % 2)
                sp.dma_start(half(raw, m, RING), win_v[:, k:k + 4, lo:hi]).then_inc(win_in[m % RING], 16)

            load_win(0)
            load_win(1)
            for j, g in enumerate((a_q_norm_g, a_k_norm_g, b_q_norm_g, b_k_norm_g)):
                for h in range(2):
                    sp.dma_start(gain_rows[j:j + 1, h * HD:(h + 1) * HD], g).then_inc(small_in, 16)
            sp.dma_start(sinks[:, :], a_sinks.to_broadcast([P, AQ])).then_inc(small_in, 16)
            sp.dma_start(br_b[:, :], b_router.to_broadcast([P, NE])).then_inc(small_in, 16)
            for m in range(2, RING):
                load_win(m)
            sp.dma_start(wr[:, :, :], w_router[0].rearrange("(k p) e -> p k e", p=P)).then_inc(router_in, 16)
            for m in range(RING, 2 * len(BLOCKS)):
                wait_half_used(sp, m - RING)
                load_win(m)

            def load_w1(e, k, c):
                e = e if isinstance(e, int) else bass.ds(e, 1)
                src = w1[0, e, k * P:(k + 1) * P, :]
                src = src if len(src.shape) == 2 else src.rearrange("e p n -> (e p) n")
                sp.dma_start(raw[:, slot(c), :], src).then_inc(raw_in[slot(c)], 16)

            def load_w2(e, k, c):
                src = w2[0, bass.ds(e, 1), k * 2 * P:(k + 1) * 2 * P, :].rearrange("e (j p) n -> p (e j) n", p=P)
                sp.dma_start(raw[:, slot(c), :].rearrange("p (j n) -> p j n", j=2), src).then_inc(raw_in[slot(c)], 16)

            def slot_free(i, c):
                sp.wait_ge(chunk_used, number(i, c) - RING + 1)

            wait_half_used(sp, 9)
            sp.dma_start(wout_sb, w_out[0].rearrange("(k p) n -> p k n", p=P)).then_inc(wout_in, 16)
            sp.wait_ge(att_turned, 2 * NT)
            for h in range(2):
                sp.dma_start(bias_raw[h * NE:(h + 1) * NE, :], b1[0]).then_inc(bias_in, 16)
            sp.wait_ge(out_done, 2 * NT)
            for k in range(RING):
                load_w1(0, k, 4 + k)
            sp.dma_start(b2_rows[:, :], b2[0]).then_inc(b2_in, 16)
            for k in range(RING, W1C):
                slot_free(0, 4 + k)
                load_w1(0, k, 4 + k)

            def iteration(i, e, before):
                for c in range(CH):
                    slot_free(i, c)
                    if c < W1C:
                        load_w1(e, c, c)
                    else:
                        load_w2(before, c - W1C, c)

            with sp.Fori(1, NE) as i:
                iteration(i, i, i - 1)
            sp.wait_ge(items_ready, 1)
            n_items = sp.value_load(items[0:1, GC - 1:GC], min_val=NE - 1, max_val=NE + OVER - 1) + 1
            with sp.If(n_items > NE):
                with sp.Fori(NE, n_items) as i:
                    e = sp.value_load(items[0:1, bass.ds(i, 1)], min_val=0, max_val=NE - 1)
                    before_e = sp.value_load(items[0:1, bass.ds(i - 1, 1)], min_val=0, max_val=NE - 1)
                    iteration(i, e, before_e)
            last_e = sp.value_load(items[0:1, bass.ds(n_items - 1, 1)], min_val=0, max_val=NE - 1)
            for c in range(CH - W1C):
                slot_free(n_items, c)
                load_w2(last_e, c, c)
            for t in range(NT):
                sp.wait_ge(acc_done, n_items * NT + (t + 1))
                sp.dma_start(out[0, t * P:(t + 1) * P, :], acc[:, t, :]).then_inc(out_stored, 16)
            sp.wait_ge(out_stored, 16 * NT)

        @block.gpsimd
        def _(pool):
            pool.memset(ident[:, :], 0.0).then_inc(pool_step, 1)
            pool.memset(before[:, :], 0.0).then_inc(pool_step, 1)
            pool.memset(half_pow[:, :], -0.5).then_inc(ident_ready, 1)
            pool.wait_ge(pool_step, 2)
            pool.affine_select(out=ident[:, :], in_=ident[:, :], compare_op=ALU.not_equal, fill=1.0, base=0,
                               pattern=[[-1, P]], channel_multiplier=1).then_inc(ident_ready, 1)
            pool.affine_select(out=before[:, :], in_=before[:, :], compare_op=ALU.is_ge, fill=1.0, base=0,
                               pattern=[[-1, P]], channel_multiplier=1).then_inc(consts_ready, 1)
            pool.memset(ones[:, :], 1.0).then_inc(ident_ready, 1)
            pool.iota(slot_iota[:, :], pattern=[[1, P]], base=0, channel_multiplier=0,
                      allow_small_or_imprecise_dtypes=True).then_inc(consts_ready, 1)
            pool.iota(e_iota[:, :], pattern=[[1, 1]], base=0, channel_multiplier=1,
                      allow_small_or_imprecise_dtypes=True).then_inc(consts_ready, 1)
            pool.iota(row_number[:, :], pattern=[[1, 1]], base=0, channel_multiplier=1,
                      allow_small_or_imprecise_dtypes=True).then_inc(consts_ready, 1)
            pool.memset(neg_ones[:, :], -1.0).then_inc(consts_ready, 1)
            pool.iota(delta_i[:, :], pattern=[[1, 896]], base=-384, channel_multiplier=-1).then_inc(delta_ready, 1)
            pool.memset(nslope[:, 2 * NP:], 0.0).then_inc(pool_step, 1)
            for r in range(NP):
                for hh in range(2):
                    head = (r + 4 * hh) if r < 4 else (8 + 2 * (r - 4) + hh)
                    pool.memset(nslope[:, 2 * r + hh:2 * r + hh + 1], -(2.0 ** (-8.0 * (head + 1) / 16))
                                ).then_inc(pool_step, 1)
            for t in range(NT):
                pool.wait_ge(var_x, t + 1)
                pool.tensor_tensor(stat[:, 8 + t:9 + t], stat[:, 4 + t:5 + t], half_pow[:, 0:1], ALU.pow
                                   ).then_inc(rstd_x, 1)
            for b in range(4):
                pool.wait_ge(var_q, b + 1)
                v = sumsq[:, b, :, 0:NORMED[b] // HD]
                pool.tensor_tensor(v, v, half_pow[:, 0:NT * (NORMED[b] // HD)].rearrange(
                    "p (t h) -> p t h", t=NT), ALU.pow).then_inc(rstd_q, 1)

            pool.wait_ge(xn_ready, NT)

            def stage(kind, it, s):
                r = it * 2 + s
                pool.wait_ge(scores_read, it * 16 + 8 * s + 8)
                if kind == "a":
                    pool.tensor_copy(q_st[:, s, :], qta[:, bass.ds(r, 1), :].rearrange("p a n -> p (a n)")
                                     ).then_inc(staged, 1)
                else:
                    pool.tensor_copy(q_st[:, s, :], qtb[:, bass.ds(r - 4, 1), :].rearrange("p a n -> p (a n)")
                                     ).then_inc(staged, 1)
                    pool.tensor_copy(k_st[:, s, :], ktb[:, bass.ds(r - 4, 1), :].rearrange("p a n -> p (a n)")
                                     ).then_inc(staged, 1)

            pool.wait_ge(qkt_copied[0], 3)
            pool.wait_ge(qkt_copied[1], 2)
            with pool.Fori(0, 2) as it:
                for s in range(2):
                    stage("a", it, s)
            pool.wait_ge(qkt_copied[0], 7)
            pool.wait_ge(qkt_copied[1], 6)
            pool.wait_ge(qkv_done, 20)
            with pool.Fori(2, 4) as it:
                for s in range(2):
                    stage("b", it, s)
                for j in range(2):
                    hi, loaded, lo = wout_split(it, j)
                    pool.wait_ge(wout_hi_done, it * 2 + (j - 3))
                    pool.tensor_tensor(lo, loaded, hi.bitcast(F32), ALU.subtract).then_inc(wout_lo_done, 1)
            for t in range(NT):
                pool.wait_ge(var_1, t + 1)
                pool.tensor_tensor(stat[:, 8 + t:9 + t], stat[:, 4 + t:5 + t], half_pow[:, 0:1], ALU.pow
                                   ).then_inc(rstd_1, 1)

            def lo_part(i, c):
                if c not in POOL_LO:
                    return
                pool.wait_ge(hi_done, number(i, c) + 1)
                pool.tensor_tensor(w_lo[:, slot(c), :], raw[:, slot(c), :], w_hi[:, slot(c), :].bitcast(F32),
                                   ALU.subtract).then_inc(lo_done[1], 1)

            def iteration(i, first=False):
                for c in range(4 if first else 0, CH):
                    lo_part(i, c)
                pool.wait_ge(prod_ready, i + 1)
                pool.wait_ge(sig_ready, i + 1)
                pool.tensor_tensor(glu[:, :], lin[:, :], sig[:, :], ALU.mult).then_inc(act_ready, 1)

            iteration(0, first=True)
            with pool.Fori(1, NE) as i:
                iteration(i)
            pool.wait_ge(items_ready, 1)
            n_items = pool.value_load(items[0:1, GC - 1:GC], min_val=NE - 1, max_val=NE + OVER - 1) + 1
            with pool.If(n_items > NE):
                with pool.Fori(NE, n_items) as i:
                    iteration(i)
            for c in range(CH - W1C):
                lo_part(n_items, c)

        @block.scalar
        def _(act):
            for t in range(NT):
                act.wait_ge(x_in[t], 16)
                if t >= 1:
                    act.wait_ge(sq_x, t)
                act.activation(xt[:, 0:2, :], acc[:, t, :].rearrange("p (a n) -> p a n", a=2), ACT.Square,
                               accum_out=stat[:, t:t + 1]).then_inc(sq_x, 1)
            def win_high(m):
                act.wait_ge(win_in[m % RING], 16 * (m // RING + 1))
                if m in (2, 3) or m >= 6:
                    wait_half_used(act, m - 2)
                elif m == 4:
                    act.wait_ge(xt_turned, 2 * NT)
                act.activation(win_high_of(m), half(raw, m, RING), ACT.Copy).then_inc(win_hi_done, 1)

            win_high(0)
            win_high(1)
            for t in range(NT):
                act.wait_ge(xt_turned, 2 * t + 2)
                act.activation(xt_hi[:, :, t * P:(t + 1) * P], bank(2 * t, 2).rearrange("p (k n) -> p k n", k=ND),
                               ACT.Copy).then_inc(xt_copied[0], 1)
            n_sq = 0

            def turn_copy(n, dst, col):
                act.wait_ge(head_ready, 1)
                act.wait_ge(qkt_turned, n + 1)
                act.activation(dst, bank(6 + n % 2), ACT.Copy, scale=head_g[:, col:col + 1]
                               ).then_inc(qkt_copied[0], 1)

            pieces = turn_pieces(qta, kta, qtb, ktb)
            for b, (lo, hi) in enumerate(BLOCKS):
                if b < 4:
                    win_high(2 * b + 2)
                for t in range(NT):
                    g = 4 * b + t
                    act.wait_ge(qkv_done, g + 1)
                    last = act.activation(paired(b, qkv[:, t, lo:hi]), banked(b, bank(g % 6)[:, 0:hi - lo]), ACT.Copy)
                    if b < 4:
                        w = NORMED[b]
                        if n_sq >= 2:
                            act.wait_ge(sq_read, n_sq - 1)
                        last = act.activation(paired(b, squares[:, n_sq % 2, 0:w]), banked(b, bank(g % 6)[:, 0:w]),
                                              ACT.Square)
                        last.then_inc(qkv_copied, 1)
                        n_sq += 1
                    else:
                        last.then_inc(qkv_copied, 1)
                    if b >= 1 and t < len(pieces[b - 1]) and pieces[b - 1][t][0] % 2 == 0:
                        turn_copy(*pieces[b - 1][t])
                if b < 4:
                    win_high(2 * b + 3)
            act.sem_inc(pt_copied[0], 1)

            def exp_unit(kind, it, u):
                i = (u % UN) // 2
                w = (keys(kind, i)[1] - keys(kind, i)[0]) * P
                act.wait_ge(max_ready, it * 16 + u + 1)
                act.activation(probs[:, u % 4, 0:w], probs[:, u % 4, 0:w], ACT.Exp, bias=neg_max[:, u:u + 1],
                               accum_out=den[:, u:u + 1]).then_inc(exp_done, 1)

            def copy_unit(kind, it, u):
                i = (u % UN) // 2
                w = (keys(kind, i)[1] - keys(kind, i)[0]) * P
                act.wait_ge(turned, it * 16 + u + 1 + 4)
                act.activation(probs_t[:, 0, 0:w], bank(4)[:, 0:w], ACT.Copy).then_inc(pt_copied[0], 1)

            def sink_exp(it, s):
                act.wait_ge(sink_d_ready, it * 2 + s + 1)
                act.activation(sink_e[:, 8 * s:8 * s + 8], sink_d[:, 8 * s:8 * s + 8], ACT.Exp
                               ).then_inc(sink_e_ready, 1)

            def attend(kind, it):
                for u in range(LEAD):
                    exp_unit(kind, it, u)
                for u in range(16):
                    if u + LEAD < 16:
                        exp_unit(kind, it, u + LEAD)
                    if u % 2 == 0:
                        copy_unit(kind, it, u)
                    if kind == "a" and u == 8:
                        sink_exp(it, 0)
                    if kind == "b" and u in (3, 5):
                        hi, loaded, _lo = wout_split(it, u // 5)
                        act.wait_ge(wout_in, 16)
                        act.activation(hi, loaded, ACT.Copy).then_inc(wout_hi_done, 1)
                if kind == "a":
                    sink_exp(it, 1)

            with act.Fori(0, 2) as it:
                attend("a", it)
            with act.Fori(2, 4) as it:
                attend("b", it)
            for t in range(NT):
                act.wait_ge(att_turned, 2 * t + 2)
                act.activation(xt_hi[:, :, t * P:(t + 1) * P], bank(2 * t, 2).rearrange("p (k n) -> p k n", k=ND),
                               ACT.Copy).then_inc(att_copied[0], 1)

            def hi_part(i, c):
                if c >= CH:
                    i, c = i + 1, c - CH
                act.wait_ge(raw_in[slot(c)], i * 32 + ((c - 4) // RING + 1) * 16)
                act.activation(w_hi[:, slot(c), :], raw[:, slot(c), :], ACT.Copy).then_inc(hi_done, 1)

            def square(t):
                act.wait_ge(x1_done, 2 * t + 2)
                if t >= 1:
                    act.wait_ge(sq_1, t)
                act.activation(norm_out[:, :, :], acc[:, t, :].rearrange("p (a n) -> p a n", a=2), ACT.Square,
                               accum_out=stat[:, t:t + 1]).then_inc(sq_1, 1)

            def copy_hf(t):
                act.wait_ge(hf_turned, 2 * t + 1)
                act.activation(xt[:, 0:4, t * P:(t + 1) * P], bank(2 * t).rearrange("p (k n) -> p k n", k=4),
                               ACT.Copy).then_inc(hf_copied[0], 1)
                act.activation(hf_hi[:, t, :], hf[:, t, :], ACT.Copy).then_inc(hf_hi_done, 1)

            square(0)
            for t in range(NT):
                if t + 1 < NT:
                    square(t + 1)
                copy_hf(t)
            act.wait_ge(bias_in, 32)
            act.activation(bias_rows[:, :], bias_raw[:, :], ACT.Copy).then_inc(bias_split_hi, 1)
            for c in range(4, 7):
                hi_part(0, c)
            act.wait_ge(gap_ready, 1)
            act.activation(top_w[:, :, :], top_w[:, :, :], ACT.Exp).then_inc(gap_exp, 1)
            def y_high(i):
                act.wait_ge(chunk_used, number(i, 0))
                act.activation(y_hi[:, :], bank(4, 2), ACT.Copy).then_inc(y_hi_done, 1)

            def act_high(i):
                act.wait_ge(act_turned, i)
                act.activation(act_hi[:, :, :], bank(6, 2).rearrange("p (k n) -> p k n", k=ND), ACT.Copy
                               ).then_inc(act_hi_done, 1)

            def sel_copy(i):
                act.wait_ge(sel_turned, i)
                act.activation(sel_t[:, :], bank(4), ACT.Copy).then_inc(sel_t_done, 1)

            def x_copy(i):
                act.wait_ge(gathered, i + 1)
                act.activation(x_tok[:, :], bank(6, 2), ACT.Copy).then_inc(x_tok_done, 1)

            def x_high(i):
                act.wait_ge(x_turned, i + 1)
                act.activation(x_hi[:, :, :], bank(6, 2).rearrange("p (k n) -> p k n", k=ND), ACT.Copy
                               ).then_inc(x_hi_done, 1)

            def sigmoid(i):
                act.wait_ge(glu_ready, i + 1)
                act.activation(sig[:, :], glu[:, :], ACT.Sigmoid, scale=ALPHA).then_inc(sig_ready, 1)

            x_copy(0)
            x_high(0)
            act.wait_ge(bias_split_lo, 1)
            for c in range(4, CH):
                hi_part(0, c + 3)
            x_copy(1)
            sigmoid(0)
            x_high(1)
            act.wait_ge(y_zeroed, 1)

            def iteration(i):
                y_high(i)
                for c in range(CH):
                    hi_part(i, c + 3)
                    if c == 1:
                        act_high(i)
                        sel_copy(i)
                    elif c == 6:
                        x_copy(i + 1)
                    elif c == 7:
                        x_high(i + 1)
                    elif c == 8:
                        sigmoid(i)

            with act.Fori(1, NE) as i:
                iteration(i)
            act.wait_ge(items_ready, 1)
            n_items = act.value_load(items[0:1, GC - 1:GC], min_val=NE - 1, max_val=NE + OVER - 1) + 1
            with act.If(n_items > NE):
                with act.Fori(NE, n_items) as i:
                    iteration(i)
            y_high(n_items)
            act_high(n_items)
            hi_part(n_items, 3)
            sel_copy(n_items)
            act.wait_ge(combined, n_items * NT)
            act.wait_ge(sel_turned, n_items + 1)
            act.activation(sel_t[:, :], bank(2), ACT.Copy).then_inc(sel_t_done, 1)
            act.wait_ge(chunk_used, n_items * CH)
            act.activation(y_hi[:, :], bank(0, 2), ACT.Copy).then_inc(y_hi_done, 1)

        @block.vector
        def _(dve):
            steps = [0]

            def step(ins):
                steps[0] += 1
                ins.then_inc(dve_step, 1)
                dve.wait_ge(dve_step, steps[0])

            dve.sem_inc(scores_read, 16)
            for n in range(2):
                dve.wait_ge(gain_rep, n + 1)
                dve.tensor_copy(gain_b[:, n, :], bank(4 + 2 * n, 2)).then_inc(gain_copied, 1)
            for t in range(NT):
                dve.wait_ge(sq_x, t + 1)
                dve.tensor_scalar(stat[:, 4 + t:5 + t], stat[:, t:t + 1], 1.0 / D, EPS, ALU.mult, ALU.add
                                  ).then_inc(var_x, 1)
            dve.wait_ge(gain_copied, 2)
            for t in range(NT):
                dve.wait_ge(rstd_x, t + 1)
                dve.scalar_tensor_tensor(out=xn[:, t, :], in0=acc[:, t, :], scalar=stat[:, 8 + t:9 + t],
                                         in1=gain_b[:, 0, :], op0=ALU.mult, op1=ALU.mult).then_inc(xn_ready, 1)
            def win_low(m):
                dve.wait_ge(win_hi_done, m + 1)
                dve.tensor_tensor(half(w_lo, m, RING), half(raw, m, RING), win_high_of(m).bitcast(F32),
                                  ALU.subtract).then_inc(win_lo_done, 1)

            win_low(0)
            win_low(1)
            for t in range(NT):
                dve.wait_ge(xt_copied[0], t + 1)
                cols = slice(t * P, (t + 1) * P)
                dve.tensor_tensor(xt_lo[:, :, cols], bank(2 * t, 2).rearrange("p (k n) -> p k n", k=ND),
                                  xt_hi[:, :, cols].bitcast(F32), ALU.subtract).then_inc(xt_copied[1], 1)
            dve.wait_ge(head_turned, 1)
            step(dve.tensor_copy(head_g[:, :], bank(0)[:, 0:4]))
            for col in (0, 2):
                last = dve.tensor_scalar(head_g[:, col:col + 1], head_g[:, col:col + 1], HD ** -0.5, None, ALU.mult)
                if col == 0:
                    step(last)
            last.then_inc(head_ready, 1)
            dve.wait_ge(delta_ready, 1)
            step(dve.tensor_copy(tmp_a[:, :], delta_i[:, :]))
            step(dve.scalar_tensor_tensor(out=dist[:, :], in0=tmp_a[:, :], scalar=-1.0, in1=tmp_a[:, :],
                                          op0=ALU.mult, op1=ALU.max))
            step(dve.tensor_scalar(logs[:, 0, :], dist[:, :], float(A_HALF), NEG, ALU.is_gt, ALU.mult))
            for n, (window, dil) in enumerate(BRANCHES):
                if dil == 1:
                    step(dve.tensor_scalar(tmp_a[:, :], dist[:, :], window / 2.0, None, ALU.is_le))
                    continue
                step(dve.tensor_scalar(low_i[:, :], delta_i[:, :], dil - 1, None, ALU.bitwise_and))
                step(dve.tensor_scalar(tmp_b[:, :], low_i[:, :], 0.0, None, ALU.is_equal))
                step(dve.scalar_tensor_tensor(out=tmp_b[:, :], in0=dist[:, :], scalar=window / 2.0, in1=tmp_b[:, :],
                                              op0=ALU.is_le, op1=ALU.mult))
                step(dve.tensor_tensor(tmp_a[:, :], tmp_a[:, :], tmp_b[:, :], ALU.add))
            win_low(2)
            step(dve.tensor_scalar(logs[:, 1, :], tmp_a[:, :], 0.0, NEG, ALU.is_equal, ALU.mult))
            for n, ln in ((2.0, LN2), (3.0, LN3)):
                step(dve.tensor_scalar(tmp_b[:, :], tmp_a[:, :], n, ln, ALU.is_equal, ALU.mult))
                last = dve.tensor_tensor(logs[:, 1, :], logs[:, 1, :], tmp_b[:, :], ALU.add)
                if n == 2.0:
                    step(last)
            last.then_inc(tables_ready, 1)

            pieces = turn_pieces(qta, kta, qtb, ktb)

            def copy_piece(b, t):
                if b >= 1 and t < len(pieces[b - 1]) and pieces[b - 1][t][0] % 2 == 1:
                    n, dst, col = pieces[b - 1][t]
                    dve.wait_ge(qkt_turned, n + 1)
                    dve.tensor_scalar(dst, bank(7), head_g[:, col:col + 1], None, ALU.mult).then_inc(qkt_copied[1], 1)

            n_sq = 0
            for b, (lo, hi) in enumerate(BLOCKS):
                if b < 4:
                    if b >= 1:
                        win_low(2 * b + 2)
                    w = NORMED[b]
                    nh = w // HD
                    for t in range(NT):
                        dve.wait_ge(qkv_copied, 4 * b + t + 1)
                        last = dve.tensor_reduce(sumsq[:, b, t, 0:nh],
                                                 squares[:, n_sq % 2, 0:w].rearrange("p (h d) -> p h d", d=HD),
                                                 AX.X, ALU.add).then_inc(sq_read, 1)
                        n_sq += 1
                        copy_piece(b, t)
                    v = sumsq[:, b, :, 0:nh]
                    dve.wait_ge(sq_read, n_sq)
                    dve.tensor_scalar(v, v, 1.0 / HD, EPS, ALU.mult, ALU.add).then_inc(var_q, 1)
                    win_low(2 * b + 3)
                    dve.wait_ge(rstd_q, b + 1)
                    for t in range(NT):
                        head = qkv[:, t, lo:lo + w].rearrange("p (h d) -> p h d", d=HD)
                        dve.tensor_tensor(head, head, sumsq[:, b, t, 0:nh].unsqueeze(2).to_broadcast([P, nh, HD]),
                                          ALU.mult).then_inc(qk_normed, 1)
                else:
                    for t in range(NT):
                        copy_piece(b, t)
            dve.sem_inc(pt_copied[1], 1)
            dve.sem_inc(o_read, 4)

            def bias_table(which, it, s, hh):
                head = it * 4 + (2 * s + hh)
                slope = nslope[:, head:head + 1] if isinstance(head, int) else nslope[:, bass.ds(head, 1)]
                log = logs[:, which, :] if isinstance(which, int) else logs[:, bass.ds(which, 1), :].rearrange(
                    "p a n -> p (a n)")
                dve.wait_ge(scores_read, it * 16 + (8 * s + 8))
                dve.scalar_tensor_tensor(out=table[:, s, hh, :], in0=dist[:, :], scalar=slope, in1=log,
                                         op0=ALU.mult, op1=ALU.add).then_inc(bias_ready, 1)

            dve.wait_ge(pool_step, 3 + 2 * NP)

            def score_unit(kind, it, u):
                s, hh, i = u // UN, u % 2, (u % UN) // 2
                k0, k1 = keys(kind, i)
                w, off = (k1 - k0) * P, (k0 - i) * P + 384
                units = dve.to_reg(it * 16 + u + 1)
                tables = dve.to_reg(it * 4 + 2 * s + hh + 1) if u % UN < 2 else None
                dve.wait_ge(tables_ready, 1)
                if u % UN < 2:
                    dve.wait_ge(bias_ready, tables)
                dve.wait_ge(scored, units)
                dve.wait_ge(turned, units)
                dve.tensor_tensor_reduce(out=probs[:, u % 4, 0:w], in0=bank(u % 4)[:, 0:w],
                                         in1=table[:, s, hh, off:off + w], scale=1.0, scalar=-3e38,
                                         op0=ALU.add, op1=ALU.max, accum_out=maxes[:, u:u + 1]
                                         ).then_inc(scores_read, 1)
                dve.wait_ge(scores_read, it * 16 + u + 1 + 16)
                if kind == "a":
                    dve.tensor_scalar(neg_max[:, u:u + 1], maxes[:, u:u + 1],
                                      sinks[:, bass.ds(it * 2 + (s + 4 * hh), 1)], -1.0, ALU.max, ALU.mult
                                      ).then_inc(max_ready, 1)
                else:
                    dve.tensor_scalar(neg_max[:, u:u + 1], maxes[:, u:u + 1], -1.0, None, ALU.mult
                                      ).then_inc(max_ready, 1)

            def copy_unit(kind, it, u):
                i = (u % UN) // 2
                w = (keys(kind, i)[1] - keys(kind, i)[0]) * P
                dve.wait_ge(turned, it * 16 + u + 1 + 4)
                dve.tensor_copy(probs_t[:, 1, 0:w], bank(5)[:, 0:w]).then_inc(pt_copied[1], 1)

            def sink_gap(it, s):
                dve.wait_ge(max_ready, it * 16 + 8 * s + 8)
                base = sinks[:, bass.ds(it * 2 + s, 5)]
                two = base.rearrange("p n -> p n")[:, 0:5:4].unsqueeze(1).to_broadcast([P, NT, 2])
                dve.tensor_tensor(sink_d[:, 8 * s:8 * s + 8].rearrange("p (i h) -> p i h", h=2),
                                  neg_max[:, 8 * s:8 * s + 8].rearrange("p (i h) -> p i h", h=2), two, ALU.add
                                  ).then_inc(sink_d_ready, 1)

            def normalise(kind, it, s):
                u8 = slice(8 * s, 8 * s + 8)
                dve.wait_ge(exp_done, it * 16 + 8 * s + 8)
                if kind == "a":
                    dve.wait_ge(sink_e_ready, it * 2 + s + 1)
                    dve.tensor_tensor(den[:, u8], den[:, u8], sink_e[:, u8], ALU.add).then_inc(den_ready, 1)
                    dve.wait_ge(den_ready, it * 2 + s + 1)
                dve.reciprocal(recip[:, u8], den[:, u8]).then_inc(recip_ready, 1)
                dve.wait_ge(recip_ready, it * 2 + s + 1)
                dve.wait_ge(pv_done, it * 2 + s + 1)
                for hh in range(2):
                    if kind == "a":
                        col = it * 2 * HD + ((s + 4 * hh) * HD + ATT)
                    else:
                        col = (it - 2) * 4 * HD + ((2 * s + hh) * HD + ATT + AQ * HD)
                    o = bank(6 + s).rearrange("p (i h d) -> p i h d", h=2, d=HD)[:, :, hh, :]
                    r = recip[:, u8].rearrange("p (i h) -> p i h", h=2)[:, :, hh:hh + 1].to_broadcast([P, NT, HD])
                    dve.tensor_tensor(qkv[:, :, bass.ds(col, HD)], o, r, ALU.mult).then_inc(o_read, 1)

            def attend(kind, it):
                def softmax_part(u):
                    if u in (5, 6):
                        bias_table(0 if kind == "a" else 1, it, 1, u - 5)
                    if u in (12, 14):
                        bias_table(it if kind == "a" else 1, it + 1, 0, (u - 12) // 2)
                    score_unit(kind, it, u)
                    if kind == "a" and u % UN == 7:
                        sink_gap(it, u // UN)

                for u in range(LEAD):
                    softmax_part(u)
                for u in range(16):
                    if u + LEAD < 16:
                        softmax_part(u + LEAD)
                    if u % 2 == 1:
                        copy_unit(kind, it, u)
                    if u == 9:
                        normalise(kind, it, 0)
                normalise(kind, it, 1)

            for hh in range(2):
                bias_table(0, 0, 0, hh)
            with dve.Fori(0, 2) as it:
                attend("a", it)
            with dve.Fori(2, 4) as it:
                attend("b", it)
            for t in range(NT):
                dve.wait_ge(att_copied[0], t + 1)
                cols = slice(t * P, (t + 1) * P)
                dve.tensor_tensor(att_lo[:, :, cols], bank(2 * t, 2).rearrange("p (k n) -> p k n", k=ND),
                                  xt_hi[:, :, cols].bitcast(F32), ALU.subtract).then_inc(att_copied[1], 1)

            def norm_token_tile(t):
                dve.wait_ge(sq_1, t + 1)
                dve.tensor_scalar(stat[:, 4 + t:5 + t], stat[:, t:t + 1], 1.0 / D, EPS, ALU.mult, ALU.add
                                  ).then_inc(var_1, 1)
                dve.wait_ge(rstd_1, t + 1)
                dve.scalar_tensor_tensor(out=hf[:, t, :], in0=acc[:, t, :], scalar=stat[:, 8 + t:9 + t],
                                         in1=gain_b[:, 1, :], op0=ALU.mult, op1=ALU.mult).then_inc(hf_ready, 1)

            def residual(t):
                for n in range(2):
                    dve.wait_ge(out_done, 2 * t + n + 1)
                    part = acc[:, t, n * 512:(n + 1) * 512]
                    dve.tensor_tensor(part, bank(2 * t + n), part, ALU.add).then_inc(x1_done, 1)

            def copy_hf(t):
                dve.wait_ge(hf_turned, 2 * t + 2)
                dve.tensor_copy(xt[:, 4:8, t * P:(t + 1) * P], bank(2 * t + 1).rearrange("p (k n) -> p k n", k=4)
                                ).then_inc(hf_copied[1], 1)
                dve.wait_ge(hf_hi_done, t + 1)
                dve.tensor_tensor(hf_lo[:, t, :], hf[:, t, :], hf_hi[:, t, :].bitcast(F32), ALU.subtract
                                  ).then_inc(hf_lo_done, 1)

            def top_four(t):
                dve.wait_ge(logits_done, t + 1)
                step(dve.tensor_tensor(logits[:, t, :], bank(2 * t)[:, 0:NE], br_b[:, :], ALU.add))
                step(dve.max(top[:, t, :], logits[:, t, :]))
                return dve.max_index(top_i[:, t, :], top[:, t, :], logits[:, t, :])

            residual(0)
            norm_token_tile(0)
            for t in range(1, NT):
                residual(t)
                norm_token_tile(t)
                copy_hf(t - 1)
                if t >= 2:
                    step(top_four(t - 2))
            copy_hf(NT - 1)
            step(top_four(NT - 2))
            step(top_four(NT - 1))
            dve.tensor_tensor(top_w[:, :, :], top[:, :, 0:TOPK], top[:, :, 0:1].to_broadcast([P, NT, TOPK]),
                              ALU.subtract).then_inc(gap_ready, 1)
            step(dve.tensor_copy(top_e[:, :, :], top_i[:, :, 0:TOPK]))
            dve.wait_ge(consts_ready, 5)
            flat_e = top_e[:, :, :].rearrange("p t j -> p (t j)").unsqueeze(2).to_broadcast([P, 16, NE])
            step(dve.tensor_tensor(chosen[:, :, :], slot_iota[:, 0:NE].unsqueeze(1).to_broadcast([P, 16, NE]), flat_e,
                                   ALU.is_equal))
            dve.tensor_reduce(mask[:, :, :], chosen[:, :, :].rearrange("p (t j) e -> p t e j", t=NT), AX.X, ALU.add
                              ).then_inc(mask_ready, 1)
            dve.wait_ge(gap_exp, 1)
            step(dve.tensor_reduce(top_s[:, :], top_w[:, :, :], AX.X, ALU.add))
            step(dve.reciprocal(top_r[:, :], top_s[:, :]))
            step(dve.tensor_tensor(top_w[:, :, :], top_w[:, :, :], top_r[:, :].unsqueeze(2).to_broadcast([P, NT, TOPK]),
                                   ALU.mult))
            step(dve.tensor_tensor(weighed[:, :, :], chosen[:, :, :],
                                   top_w[:, :, :].rearrange("p t j -> p (t j)").unsqueeze(2).to_broadcast([P, 16, NE]),
                                   ALU.mult))
            step(dve.memset(gate_t[:, :, :], 0.0))
            step(dve.tensor_reduce(gate_t[:, :, 2:NE + 2], weighed[:, :, :].rearrange("p (t j) e -> p t e j", t=NT),
                                   AX.X, ALU.add))
            step(dve.memset(pos_t[:, :, :], -1.0))
            dve.wait_ge(pos_done, 1)
            step(dve.scalar_tensor_tensor(out=weighed[:, 0:NT, :], in0=bank(1)[:, 0:NT * NE].rearrange(
                "p (t e) -> p t e", t=NT), scalar=1.0, in1=mask[:, :, :], op0=ALU.add, op1=ALU.mult))
            step(dve.tensor_scalar(pos_t[:, :, 2:NE + 2], weighed[:, 0:NT, :], -1.0, None, ALU.add))

            def select_bias(dst, i):
                row = item_row[:, bass.ds(i, 1)] if not isinstance(i, int) else item_row[:, i:i + 1]
                dve.tensor_tensor(dst[:, :], row_number[:, :].to_broadcast([2 * NE, P]), row.to_broadcast([2 * NE, P]),
                                  ALU.is_equal).then_inc(bias_sel_ready, 1)

            dve.wait_ge(hf_copied[0], NT)
            dve.wait_ge(logits_done, NT)
            dve.wait_ge(hf_lo_done, NT)
            def select(dst, col, done):
                place = pos_t[:, :, bass.ds(col, 1)] if not isinstance(col, int) else pos_t[:, :, col:col + 1]
                dve.tensor_tensor(dst[:, :, :], slot_iota[:, :].unsqueeze(1).to_broadcast([P, NT, P]),
                                   place.to_broadcast([P, NT, P]), ALU.is_equal).then_inc(done, 1)

            select(sel, 2, sel_ready)
            low = slice(NE, 2 * NE)
            dve.wait_ge(bias_split_hi, 1)
            dve.tensor_tensor(bias_rows[low, :], bias_raw[low, :], bias_rows[low, :].bitcast(F32), ALU.subtract
                              ).then_inc(bias_split_lo, 1)
            step(dve.tensor_copy(item_row[0:NE, :], slot_iota[0:NE, 0:GC]))
            step(dve.tensor_scalar(item_row[low, :], slot_iota[low, 0:GC], float(NE), None, ALU.add))
            select_bias(bias_sel, 0)
            dve.wait_ge(count_done, 1)
            step(dve.tensor_copy(count[:, :], ps[0:NE, 4 * 512:4 * 512 + 1]))
            step(dve.tensor_scalar(more[:, 0:1], count[:, :], float(P), None, ALU.is_gt))
            for n in (2, 3):
                step(dve.scalar_tensor_tensor(out=more[:, 0:1], in0=count[:, :], scalar=float(n * P), in1=more[:, 0:1],
                                              op0=ALU.is_gt, op1=ALU.add))
            dve.sem_inc(more_ready, 1)
            def lo_part(i, c):
                if c >= CH:
                    i, c = i + 1, c - CH
                if c in POOL_LO:
                    return
                dve.wait_ge(hi_done, number(i, c) + 1)
                dve.tensor_tensor(w_lo[:, slot(c), :], raw[:, slot(c), :], w_hi[:, slot(c), :].bitcast(F32),
                                  ALU.subtract).then_inc(lo_done[0], 1)

            def y_low(i):
                dve.wait_ge(y_hi_done, i)
                dve.tensor_tensor(y_lo[:, :], bank(4, 2), y_hi[:, :].bitcast(F32), ALU.subtract
                                  ).then_inc(y_lo_done, 1)

            def act_low(i):
                dve.wait_ge(act_hi_done, i)
                dve.tensor_tensor(act_lo[:, :, :], bank(6, 2).rearrange("p (k n) -> p k n", k=ND),
                                  act_hi[:, :, :].bitcast(F32), ALU.subtract).then_inc(act_lo_done, 1)

            def x_low(i):
                dve.wait_ge(x_hi_done, i + 1)
                dve.tensor_tensor(x_lo[:, :, :], bank(6, 2).rearrange("p (k n) -> p k n", k=ND),
                                  x_hi[:, :, :].bitcast(F32), ALU.subtract).then_inc(x_lo_done, 1)

            def accumulate(i, t):
                dve.wait_ge(combined, i * NT + (t - 3))
                dve.scalar_tensor_tensor(out=acc[:, t, :], in0=bank(6 - 2 * (t % 2), 2), scalar=gate_t[:, t, bass.ds(i, 1)],
                                         in1=acc[:, t, :], op0=ALU.mult, op1=ALU.add).then_inc(acc_done, 1)

            def clamp_glu(i):
                dve.wait_ge(chunk_used, 8 if isinstance(i, int) else number(i, W1C))
                dve.tensor_scalar(glu[:, :], bank(0, 2), LIMIT, None, ALU.min).then_inc(glu_ready, 1)

            def clamp_lin(i):
                dve.tensor_scalar(lin[:, :], bank(2, 2), LIMIT, -LIMIT, ALU.min, ALU.max).then_inc(lin_ready, 1)
                dve.wait_ge(lin_ready, i + 1)
                dve.wait_ge(glu_ready, i + 1)
                dve.scalar_tensor_tensor(out=lin[:, :], in0=lin[:, :], scalar=1.0, in1=glu[:, :],
                                         op0=ALU.add, op1=ALU.mult).then_inc(prod_ready, 1)

            def next_biases(i):
                dve.wait_ge(bias_used, i + 1)
                select_bias(bias_sel, i + 1)

            def next_gather(i):
                dve.wait_ge(gathered, i + 1)
                select(sel, i + 3, sel_ready)

            def next_spread(i):
                dve.wait_ge(sel_turned, i)
                select(sel_c, i + 1, sel_c_ready)

            def place_items():
                dve.wait_ge(e_turned, 1)
                step(dve.tensor_copy(pos_e[:, :], ps[0:NE, 4 * 512:5 * 512]))
                step(dve.tensor_copy(gate_e[:, :], ps[0:NE, 5 * 512:6 * 512]))
                dve.wait_ge(first_done, 1)
                step(dve.tensor_copy(more[:, 1:2], ps[0:NE, 6 * 512:6 * 512 + 1]))
                step(dve.tensor_tensor(more[:, 2:3], more[:, 0:1], more[:, 1:2], ALU.add))
                v = slot_iota[0:NE, 0:OVER]
                step(dve.tensor_scalar(item_tm[:, :], v, more[:, 2:3], None, ALU.is_lt))
                step(dve.scalar_tensor_tensor(out=item_in[:, :], in0=v, scalar=more[:, 1:2], in1=item_tm[:, :],
                                              op0=ALU.is_ge, op1=ALU.mult))
                step(dve.tensor_scalar(item_tm[:, :], v, more[:, 1:2], 1.0, ALU.subtract, ALU.add))
                step(dve.scalar_tensor_tensor(out=item_sh[:, :], in0=item_tm[:, :], scalar=float(P), in1=item_in[:, :],
                                              op0=ALU.mult, op1=ALU.mult))
                dve.sem_inc(lists_ready, 1)

            def list_items():
                dve.wait_ge(over_done, 1)
                step(dve.tensor_copy(pos_t[:, :, NE + 2:NE + 2 + OVER], bank(4)[:, 0:NT * OVER].rearrange("p (t v) -> p t v", t=NT)))
                step(dve.tensor_copy(gate_t[:, :, NE + 2:NE + 2 + OVER],
                                     bank(5)[:, 0:NT * OVER].rearrange("p (t v) -> p t v", t=NT)))
                step(dve.tensor_copy(item_f[:, :], slot_iota[0:1, 0:GC]))
                step(dve.tensor_copy(item_f[:, NE:NE + OVER], ps[0:1, 6 * 512:6 * 512 + OVER]))
                step(dve.tensor_scalar(item_f[:, GC - 1:GC], ps[0:1, 6 * 512 + OVER:6 * 512 + OVER + 1], NE - 1.0, None,
                                       ALU.add))
                step(dve.tensor_copy(item_row[0:NE, NE:NE + OVER], ps[0:NE, 7 * 512:7 * 512 + OVER]))
                step(dve.tensor_scalar(item_row[low, NE:NE + OVER], ps[low, 7 * 512:7 * 512 + OVER], float(NE), None,
                                       ALU.add))
                dve.tensor_copy(items[:, :], item_f[:, :]).then_inc(items_ready, 1)


            lo_part(0, 4)
            lo_part(0, 5)
            x_low(0)
            for c in range(4, CH):
                lo_part(0, c + 2)
                if c == 5:
                    next_gather(0)
                    select(sel_c, 1, sel_c_ready)
                    place_items()
                if c == 7:
                    list_items()
                if c >= 8:
                    t = c - 8
                    dve.wait_ge(b2_spread, t + 1)
                    dve.tensor_tensor(acc[:, t, :], bank(4, 2), acc[:, t, :], ALU.add).then_inc(b2_added, 1)
            dve.wait_ge(b2_added, NT)
            dve.memset(bank(4, 2), 0.0).then_inc(y_zeroed, 1)
            clamp_glu(0)
            clamp_lin(0)
            x_low(1)
            next_biases(0)

            def iteration(i):
                y_low(i)
                for c in range(CH):
                    lo_part(i, c + 2)
                    if c == 1:
                        act_low(i)
                    elif 2 <= c < 6:
                        accumulate(i, c - 2)
                        if c == 4:
                            next_gather(i)
                    elif c == 6:
                        next_spread(i)
                    elif c == 7:
                        clamp_glu(i)
                    elif c == 8:
                        clamp_lin(i)
                    elif c == 9:
                        x_low(i + 1)
                next_biases(i)

            with dve.Fori(1, NE) as i:
                iteration(i)
            n_items = dve.value_load(items[0:1, GC - 1:GC], min_val=NE - 1, max_val=NE + OVER - 1) + 1
            with dve.If(n_items > NE):
                with dve.Fori(NE, n_items) as i:
                    iteration(i)
            y_low(n_items)
            act_low(n_items)
            lo_part(n_items, 2)
            lo_part(n_items, 3)
            next_spread(n_items)
            for t in range(NT):
                accumulate(n_items, t)
            dve.wait_ge(y_hi_done, n_items + 1)
            dve.tensor_tensor(y_lo[:, :], bank(0, 2), y_hi[:, :].bitcast(F32), ALU.subtract).then_inc(y_lo_done, 1)
            for t in range(NT):
                accumulate(n_items + 1, t)

        @block.tensor
        def _(pe):
            pe.wait_ge(rows_in, 32)
            pe.wait_ge(ident_ready, 3)
            for n in range(2):
                for h in range(2):
                    last = pe.matmul(bank(4 + 2 * n + h), ones[0:1, :], rows[0:1, n, h * 512:(h + 1) * 512],
                                     start=True, stop=True)
                last.then_inc(gain_rep, 1)
            for t in range(NT):
                pe.wait_ge(xn_ready, t + 1)
                if t >= 2:
                    pe.wait_ge(gain_copied, t - 1)
                for h in range(2):
                    for k in range(4):
                        last = pe.transpose(bank(2 * t + h)[:, k * P:(k + 1) * P],
                                            xn[:, t, (4 * h + k) * P:(4 * h + k + 1) * P], ident[:, :])
                    last.then_inc(xt_turned, 1)
            pe.wait_ge(small_in, 160)
            pe.wait_ge(xt_copied[1], 1)
            pe.transpose(bank(0)[:, 0:4], gain_rows[:, :], ident[0:4, 0:4]).then_inc(head_turned, 1)

            def turn_piece(b, n, j):
                pe.wait_ge(qk_normed, 4 * (b + 1))
                if n >= 2:
                    pe.wait_ge(qkt_copied[n % 2], n // 2)
                for t in range(NT):
                    c = BLOCKS[b][0] + j * P
                    last = pe.transpose(bank(6 + n % 2)[:, t * P:(t + 1) * P], qkv[:, t, c:c + P], ident[:, :])
                last.then_inc(qkt_turned, 1)

            pieces = turn_pieces(qta, kta, qtb, ktb)
            for b, (lo, hi) in enumerate(BLOCKS):
                for h in range(2):
                    m = 2 * b + h
                    pe.wait_ge(win_lo_done, m + 1)
                    for t in range(NT):
                        g = 4 * b + t
                        if m == 0:
                            pe.wait_ge(xt_copied[1], t + 1)
                            if t == 0:
                                pe.wait_ge(head_ready, 1)
                        if h == 0 and g >= 6:
                            pe.wait_ge(qkv_copied, g - 5)
                        tokens_t = slice(t * P, (t + 1) * P)
                        for k in range(4):
                            passes = ((xt_hi, win_high_of(m)), (xt_hi, half(w_lo, m, RING)),
                                      (xt_lo, win_high_of(m)))
                            for n, (lhs, rhs) in enumerate(passes):
                                last = pe.matmul(bank(g % 6)[:, 0:hi - lo], lhs[:, 4 * h + k, tokens_t], rhs[:, k, :],
                                                 start=(h == 0 and k == 0 and n == 0),
                                                 stop=(h == 1 and k == 3 and n == 2))
                        if h == 1:
                            last.then_inc(qkv_done, 1)
                            if b >= 1 and t < len(pieces[b - 1]):
                                turn_piece(b - 1, pieces[b - 1][t][0], t)
                        elif t == NT - 1:
                            last.then_inc(half_used, 1)

            pe.sem_inc(turned, 4)
            pe.wait_ge(qkv_copied, 19)

            def score(kind, it, u):
                s, hh, i = u // UN, u % 2, (u % UN) // 2
                k0, k1 = keys(kind, i)
                if u % UN == 0:
                    pe.wait_ge(staged, (it * 2 + s + 1) if kind == "a" else (it * 4 + 2 * s - 2))
                if u == 1:
                    pe.wait_ge(qkv_copied, 20)
                pe.wait_ge(scores_read, it * 16 + u + 13)
                kt = kta[:, :] if kind == "a" else k_st[:, s, :]
                pe.matmul(bank(u % 4)[:, 0:(k1 - k0) * P], q_st[hh * HD:(hh + 1) * HD, s, i * P:(i + 1) * P],
                          kt[hh * HD:(hh + 1) * HD, k0 * P:k1 * P], start=True, stop=True).then_inc(scored, 1)

            def turn(kind, it, u):
                i = (u % UN) // 2
                k0, k1 = keys(kind, i)
                pe.wait_ge(exp_done, it * 16 + u + 1)
                pe.wait_ge(pt_copied[u % 2], it * 8 + u // 2 + 1)
                for k in range(k1 - k0):
                    last = pe.matmul(bank(4 + u % 2)[:, k * P:(k + 1) * P], probs[:, u % 4, k * P:(k + 1) * P],
                                     ident[:, :], start=True, stop=True)
                last.then_inc(turned, 1)

            def values(kind, it, u):
                s, hh, i = u // UN, u % 2, (u % UN) // 2
                k0, k1 = keys(kind, i)
                pe.wait_ge(pt_copied[u % 2], it * 8 + u // 2 + 2)
                if u % UN == 0:
                    pe.wait_ge(o_read, it * 4 + 2 * s + 2)
                for k in range(k0, k1):
                    if kind == "a":
                        v = qkv[:, k, VA + hh * HD:VA + (hh + 1) * HD]
                    else:
                        v = qkv[:, k, bass.ds((it - 2) * 4 * HD + ((2 * s + hh) * HD + VB), HD)]
                    last = pe.matmul(bank(6 + s)[:, (u % UN) * HD:(u % UN + 1) * HD],
                                     probs_t[:, u % 2, (k - k0) * P:(k - k0 + 1) * P], v,
                                     start=(k == k0), stop=(k == k1 - 1))
                if u % UN == UN - 1:
                    last.then_inc(pv_done, 1)

            def attend(kind, it):
                for u in range(4):
                    score(kind, it, u)
                for u in range(16):
                    turn(kind, it, u)
                    if u + 4 < 16:
                        score(kind, it, u + 4)
                    if u >= 1:
                        values(kind, it, u - 1)
                values(kind, it, 15)

            with pe.Fori(0, 2) as it:
                attend("a", it)
            with pe.Fori(2, 4) as it:
                attend("b", it)

            pe.wait_ge(o_read, 2 * NP + 4)
            pe.wait_ge(scores_read, NP * UN + 16)
            for p in range(2):
                pe.wait_ge(pt_copied[p], NP * UN // 2 + 1)
            for t in range(NT):
                for h in range(2):
                    for k in range(4):
                        c = ATT + (4 * h + k) * P
                        last = pe.transpose(bank(2 * t + h)[:, k * P:(k + 1) * P], qkv[:, t, c:c + P], ident[:, :])
                    last.then_inc(att_turned, 1)
            pe.wait_ge(router_in, 16)

            def project_out(t):
                pe.wait_ge(att_copied[1], t + 1)
                for n in range(2):
                    for k in range(ND):
                        c, cols = k // 2, slice((k % 2) * D + n * 512, (k % 2) * D + (n + 1) * 512)
                        if t == 0 and n == 0 and k == 0:
                            pe.wait_ge(wout_lo_done, 4)
                        passes = ((xt_hi, wout_hi(c)), (xt_hi, w_lo[:, 2 + c, :]), (att_lo, wout_hi(c)))
                        for m, (lhs, rhs) in enumerate(passes):
                            last = pe.matmul(bank(2 * t + n), lhs[:, k, t * P:(t + 1) * P], rhs[:, cols],
                                             start=(k == 0 and m == 0), stop=(k == ND - 1 and m == 2))
                    last.then_inc(out_done, 1)

            def turn_hf(t):
                pe.wait_ge(hf_ready, t + 1)
                for h in range(2):
                    for k in range(4):
                        last = pe.transpose(bank(2 * t + h)[:, k * P:(k + 1) * P],
                                            hf[:, t, (4 * h + k) * P:(4 * h + k + 1) * P], ident[:, :])
                    last.then_inc(hf_turned, 1)

            def route(t):
                pe.wait_ge(hf_copied[0], t + 1)
                pe.wait_ge(hf_copied[1], t + 1)
                for k in range(ND):
                    last = pe.matmul(bank(2 * t)[:, 0:NE], xt[:, k, t * P:(t + 1) * P], wr[:, k, :],
                                     start=(k == 0), stop=(k == ND - 1))
                last.then_inc(logits_done, 1)

            project_out(0)
            project_out(1)
            turn_hf(0)
            project_out(2)
            route(0)
            turn_hf(1)
            project_out(3)
            route(1)
            turn_hf(2)
            route(2)
            turn_hf(3)
            route(3)
            pe.wait_ge(mask_ready, 1)
            for t in range(NT):
                for s in range(t + 1):
                    last = pe.matmul(bank(1)[:, t * NE:(t + 1) * NE], (before if s == t else ones)[:, :], mask[:, s, :],
                                     start=(s == 0), stop=(s == t))
            last.then_inc(pos_done, 1)
            for t in range(NT):
                last = pe.matmul(ps[0:NE, 4 * 512:4 * 512 + 1], mask[:, t, :], ones[:, 0:1],
                                 start=(t == 0), stop=(t == NT - 1))
            last.then_inc(count_done, 1)
            def turn_selection(sel_src, b=4):
                for t in range(NT):
                    last = pe.transpose(bank(b)[:, t * P:(t + 1) * P], sel_src[:, t, :].bitcast(F32), ident[:, :])
                last.then_inc(sel_turned, 1)

            def gather(i):
                pe.wait_ge(sel_ready, i + 1)
                for n in range(2):
                    for t in range(NT):
                        for src in (hf_hi, hf_lo):
                            last = pe.matmul(bank(6 + n), sel[:, t, :], src[:, t, n * 512:(n + 1) * 512],
                                             start=(t == 0 and src is hf_hi), stop=(t == NT - 1 and src is hf_lo))
                last.then_inc(gathered, 1)

            def turn_scratch(src, done):
                for k in range(ND):
                    last = pe.transpose(bank(6 + k // 4)[:, (k % 4) * P:(k % 4 + 1) * P], src[:, k * P:(k + 1) * P],
                                        ident[:, :])
                last.then_inc(done, 1)

            gather(0)
            pe.wait_ge(x_tok_done, 1)
            turn_scratch(x_tok, x_turned)
            pe.wait_ge(bias_split_lo, 1)

            def chunk(i, c, banks, lhs_hi, lhs_lo, pieces, begin, end):
                pool = c in POOL_LO
                pe.wait_ge(lo_done[pool], split_count(i, c, pool))
                for j, k in enumerate(pieces):
                    for m, (lhs, rhs) in enumerate(((lhs_hi, w_hi), (lhs_hi, w_lo), (lhs_lo, w_hi))):
                        for n, b in enumerate(banks):
                            cols = slice((j * len(banks) + n) * 512, (j * len(banks) + n + 1) * 512)
                            last = pe.matmul(bank(b), lhs[:, k, :], rhs[:, slot(c), cols],
                                             start=(begin and j == 0 and m == 0),
                                             stop=(end and j == len(pieces) - 1 and m == 2))
                last.then_inc(chunk_used, 1)

            def first_product(i, c0_, between):
                pe.wait_ge(x_lo_done, i + 1)
                for n in range(4):
                    last = pe.matmul(bank(n), bias_sel[:, :], bias_rows[:, n * 512:(n + 1) * 512], start=True, stop=False)
                last.then_inc(bias_used, 1)
                for k in range(W1C):
                    chunk(i, c0_ + k, range(4), x_hi, x_lo, (k,), False, k == W1C - 1)
                    between(k)

            def second_product(i, c0_, banks=(4, 5), between=lambda k: None):
                for k in range(CH - W1C):
                    chunk(i, c0_ + k, banks, act_hi, act_lo, (2 * k, 2 * k + 1), k == 0, k == CH - W1C - 1)
                    between(k)

            def turn_act(i):
                pe.wait_ge(act_ready, i)
                turn_scratch(glu, act_turned)

            def turn_sel_c(i):
                pe.wait_ge(y_lo_done, i)
                pe.wait_ge(sel_c_ready, i)
                turn_selection(sel_c)

            def combine(i, t, last_one=False):
                if t == 0:
                    pe.wait_ge(sel_t_done, i)
                    if not last_one:
                        pe.wait_ge(act_lo_done, i)
                if t >= 2 or last_one:
                    pe.wait_ge(acc_done, i * NT + (t - 5))
                for src in (y_hi, y_lo):
                    for n in range(2):
                        last = pe.matmul(bank(6 - 2 * (t % 2) + n), sel_t[:, t * P:(t + 1) * P],
                                         src[:, n * 512:(n + 1) * 512], start=(src is y_hi), stop=(src is y_lo))
                last.then_inc(combined, 1)

            def tokens(i, k):
                if k == 6:
                    gather(i)
                elif k == 7:
                    pe.wait_ge(x_tok_done, i + 1)
                    turn_scratch(x_tok, x_turned)

            def place_items():
                pe.wait_ge(more_ready, 1)
                for j, src in ((4, pos_t[:, :, 2:NE + 2]), (5, gate_t[:, :, 2:NE + 2])):
                    for t in range(NT):
                        last = pe.transpose(bank(j)[0:NE, t * P:(t + 1) * P], src[:, t, :], ident[:, :])
                last.then_inc(e_turned, 1)
                pe.matmul(ps[0:NE, 6 * 512:6 * 512 + 1], before[0:NE, 0:NE], more[:, 0:1], start=True, stop=True
                          ).then_inc(first_done, 1)

            def list_items():
                pe.wait_ge(lists_ready, 1)
                for t in range(NT):
                    o = bank(4)[:, t * OVER:(t + 1) * OVER]
                    pe.matmul(o, pos_e[:, t * P:(t + 1) * P], item_in[:, :], start=True, stop=False)
                    pe.matmul(o, neg_ones[:, :], item_sh[:, :], start=False, stop=True)
                    pe.matmul(bank(5)[:, t * OVER:(t + 1) * OVER], gate_e[:, t * P:(t + 1) * P], item_in[:, :],
                              start=True, stop=True)
                pe.matmul(ps[0:1, 6 * 512:6 * 512 + OVER], e_iota[:, :], item_in[:, :], start=True, stop=True)
                pe.matmul(ps[0:1, 6 * 512 + OVER:6 * 512 + OVER + 1], ones[0:NE, 0:1], more[:, 0:1], start=True, stop=True
                          )
                pe.matmul(ps[0:2 * NE, 7 * 512:7 * 512 + OVER], e_iota[:, :].to_broadcast([NE, 2 * NE]), item_in[:, :],
                          start=True, stop=True).then_inc(over_done, 1)

            def spread_b2(t):
                if t == 0:
                    pe.wait_ge(b2_in, 16)
                    pe.wait_ge(items_ready, 1)
                else:
                    pe.wait_ge(b2_added, t)
                for n in range(2):
                    last = pe.matmul(bank(4 + n), gate_e[:, t * P:(t + 1) * P], b2_rows[:, n * 512:(n + 1) * 512],
                                     start=True, stop=True)
                last.then_inc(b2_spread, 1)

            def between_first(k):
                if k == 0:
                    place_items()
                elif k == 3:
                    list_items()
                if k >= 4:
                    spread_b2(k - 4)
                if k >= 6:
                    tokens(1, k)

            first_product(0, 4, between_first)

            def iteration(i):
                pe.wait_ge(bias_sel_ready, i + 1)
                pe.wait_ge(lin_ready, i)

                def between(k):
                    if k == 0:
                        turn_act(i)
                    elif k == 1:
                        turn_sel_c(i)
                    elif k < 6:
                        combine(i, k - 2)
                    else:
                        if k == 6:
                            pe.wait_ge(acc_done, i * NT - 1)
                        tokens(i + 1, k)

                first_product(i, 0, between)
                pe.wait_ge(acc_done, i * NT)
                second_product(i, W1C)

            with pe.Fori(1, NE) as i:
                iteration(i)
            pe.wait_ge(items_ready, 1)
            n_items = pe.value_load(items[0:1, GC - 1:GC], min_val=NE - 1, max_val=NE + OVER - 1) + 1
            with pe.If(n_items > NE):
                with pe.Fori(NE, n_items) as i:
                    iteration(i)
            pe.wait_ge(lin_ready, n_items)
            pe.wait_ge(x_lo_done, n_items + 1)
            turn_act(n_items)
            pe.wait_ge(act_lo_done, n_items)

            def between_last(k):
                if k == 0:
                    turn_sel_c(n_items)
                elif k == 1:
                    combine(n_items, 0)
                    combine(n_items, 1)
                elif k == 2:
                    combine(n_items, 2)
                    combine(n_items, 3)
                    pe.wait_ge(sel_c_ready, n_items + 1)
                    turn_selection(sel_c, 2)

            second_product(n_items, 0, (0, 1), between_last)
            pe.wait_ge(y_lo_done, n_items + 1)
            for t in range(NT):
                combine(n_items + 1, t, last_one=True)


def turn_pieces(qta, kta, qtb, ktb):
    return (
        [(0, kta[:, :], 1)],
        [(1 + j, qta[:, j, :], 0) for j in range(4)],
        [(5 + j, qtb[:, j, :], 2) for j in range(4)],
        [(9 + j, ktb[:, j, :], 3) for j in range(4)],
    )


_INS = ["x", "attn_norm_g", "w_in", "a_q_norm_g", "a_k_norm_g", "a_sinks", "b_q_norm_g", "b_k_norm_g",
        "w_out", "ffn_norm_g", "w_router", "b_router", "w1", "b1", "w2", "b2"]


def kernel(**inputs):
    import numpy as np
    import concourse.bacc as bacc
    from concourse.bass_utils import run_bass_kernel_spmd

    nc = bacc.Bacc("TRN2", target_bir_lowering=False, num_devices=1, dynamic_dma_scratch_size=64)
    arrays, args = {}, []
    for name in _INS:
        a = np.ascontiguousarray(inputs[name])
        arrays[f"in_{name}"] = a
        args.append(nc.dram_tensor(f"in_{name}", a.shape, mybir.dt.from_np(a.dtype), kind="ExternalInput").ap())
    out = nc.dram_tensor("out", (1, SEQ, D), F32, kind="ExternalOutput").ap()
    layer(nc, *args, out)
    r = run_bass_kernel_spmd(nc, [arrays], core_ids=[0])
    return r.results[0]["out"]
```
